# Optimizing a Trainium2 kernel written in Bass

```python
import jax, jax.numpy as jnp
from jax import lax
import numpy as np

D_MODEL = 1024
BATCH = 1
SEQ = 512
DEPTH = 2

GRID_W = 64
CTX_LEN = 256
HEAD_DIM = 64
N_HEADS_A = 8
N_KV_A = 2
N_HEADS_B = 8
N_KV_B = 2
BRANCH_WIDTH = 512
CONV_K = 3
WINDOW = 128
Q_BLOCK = 128
N_BRANCH = 3
N_EXPERTS = 16
EXPERT_HIDDEN = 1024
CAPACITY_FACTOR = 2
ROPE_BASE = 10000.0
EPS = 1e-6
NEG_INF = -1e30

KV_A = N_KV_A * HEAD_DIM
KV_B = N_KV_B * HEAD_DIM
KV_END = 2 * KV_A + 2 * KV_B
OFF_QA = KV_END
OFF_QB = OFF_QA + N_HEADS_A * HEAD_DIM
OFF_CONV = OFF_QB + N_HEADS_B * HEAD_DIM
OFF_GATE = OFF_CONV + 3 * BRANCH_WIDTH
PROJ_WIDTH = OFF_GATE + N_BRANCH * D_MODEL


def rmsnorm(x, g):
    x32 = x.astype(jnp.float32)
    y = x32 * lax.rsqrt(jnp.mean(x32 * x32, axis=-1, keepdims=True) + EPS)
    return (y * g.astype(jnp.float32)).astype(x.dtype)

def modulate(h, shift, scale):
    return h * (1 + scale) + shift

def rope_tables(n):
    rows = n // GRID_W
    row = jnp.repeat(jnp.arange(rows, dtype=jnp.float32), GRID_W)
    col = jnp.tile(jnp.arange(GRID_W, dtype=jnp.float32), rows)
    n_freq = HEAD_DIM // 4
    inv = ROPE_BASE ** (-jnp.arange(n_freq, dtype=jnp.float32) / n_freq)
    ang = jnp.concatenate([row[:, None] * inv, col[:, None] * inv], axis=-1)
    return jnp.cos(ang), jnp.sin(ang)

def apply_rope(x, cos, sin):
    half = HEAD_DIM // 2
    c = cos[None, :, None, :].astype(x.dtype)
    s = sin[None, :, None, :].astype(x.dtype)
    x1, x2 = x[..., :half], x[..., half:]
    return jnp.concatenate([x1 * c - x2 * s, x2 * c + x1 * s], axis=-1)

def q_heads(p_q, qg, n_heads, n_kv, rope):
    B, n, _ = p_q.shape
    q = rmsnorm(p_q.reshape(B, n, n_heads, HEAD_DIM), qg)
    if rope is not None:
        q = apply_rope(q, *rope)
    return q.reshape(B, n, n_kv, n_heads // n_kv, HEAD_DIM)

def kv_heads(p_kv, kg_a, kg_b, rope):
    B, n, _ = p_kv.shape
    ka, va, kb, vb = jnp.split(p_kv, [KV_A, 2 * KV_A, 2 * KV_A + KV_B], axis=-1)
    ka = rmsnorm(ka.reshape(B, n, N_KV_A, HEAD_DIM), kg_a)
    kb = rmsnorm(kb.reshape(B, n, N_KV_B, HEAD_DIM), kg_b)
    va = va.reshape(B, n, N_KV_A, HEAD_DIM)
    vb = vb.reshape(B, n, N_KV_B, HEAD_DIM)
    if rope is not None:
        ka = apply_rope(ka, *rope)
        kb = apply_rope(kb, *rope)
    return ka, va, kb, vb

def attend(q, k, v, mask, sink):
    s = jnp.einsum('bqkgd,bskd->bkgqs', q, k, preferred_element_type=jnp.float32) * (HEAD_DIM ** -0.5)
    if mask is not None:
        s = jnp.where(mask, s, NEG_INF)
    if sink is not None:
        sk = jnp.broadcast_to(sink.astype(jnp.float32)[None, :, :, None, None], s.shape[:-1] + (1,))
        p = jax.nn.softmax(jnp.concatenate([s, sk], axis=-1), axis=-1)[..., :-1]
    else:
        p = jax.nn.softmax(s, axis=-1)
    return jnp.einsum('bkgqs,bskd->bqkgd', p.astype(v.dtype), v)

def to_blocks(q):
    B, n, KV, G, d = q.shape
    return q.reshape(B, n // Q_BLOCK, Q_BLOCK, KV, G, d).transpose(1, 0, 2, 3, 4, 5)

def from_blocks(o, n):
    nblk, B, qb, KV, G, d = o.shape
    return o.transpose(1, 0, 2, 3, 4, 5).reshape(B, n, KV * G * d)

def global_attention(q, k_lat, v_lat, k_ctx, v_ctx):
    k = jnp.concatenate([k_lat, k_ctx], axis=1)
    v = jnp.concatenate([v_lat, v_ctx], axis=1)
    o = lax.map(lambda qb: attend(qb, k, v, None, None), to_blocks(q))
    return from_blocks(o, q.shape[1])

def window_attention(q, k_lat, v_lat, k_ctx, v_ctx, sink):
    n = q.shape[1]
    nblk = n // Q_BLOCK
    pad = ((0, 0), (WINDOW, WINDOW), (0, 0), (0, 0))
    k_pad = jnp.pad(k_lat, pad)
    v_pad = jnp.pad(v_lat, pad)
    span = Q_BLOCK + 2 * WINDOW
    ctx_mask = jnp.ones((Q_BLOCK, k_ctx.shape[1]), dtype=bool)

    def block(args):
        i, qb = args
        start = i * Q_BLOCK
        kb = lax.dynamic_slice_in_dim(k_pad, start, span, axis=1)
        vb = lax.dynamic_slice_in_dim(v_pad, start, span, axis=1)
        qpos = start + jnp.arange(Q_BLOCK)
        kpos = start - WINDOW + jnp.arange(span)
        local = (jnp.abs(qpos[:, None] - kpos[None, :]) <= WINDOW) & (kpos >= 0)[None, :] & (kpos < n)[None, :]
        mask = jnp.concatenate([local, ctx_mask], axis=1)
        return attend(qb, jnp.concatenate([kb, k_ctx], axis=1), jnp.concatenate([vb, v_ctx], axis=1), mask, sink)

    o = lax.map(block, (jnp.arange(nblk), to_blocks(q)))
    return from_blocks(o, n)

def short_conv(p_conv, w):
    b_gate, c_gate, x_in = jnp.split(p_conv, 3, axis=-1)
    u = c_gate * x_in
    n = u.shape[1]
    up = jnp.pad(u, ((0, 0), (CONV_K // 2, CONV_K // 2), (0, 0)))
    conv = sum(w[j] * up[:, j:j + n] for j in range(CONV_K))
    return b_gate * conv

def merge_branches(o_a, o_b, o_c, gate_logits, w_branch, w_out):
    g_a, g_b, g_c = jnp.split(jax.nn.sigmoid(gate_logits), 3, axis=-1)
    merged = g_a * (o_a @ w_branch[0]) + g_b * (o_b @ w_branch[1]) + g_c * (o_c @ w_branch[2])
    return merged @ w_out

def latent_mixer(p, ctx_kv, rope, qg_a, kg_a, qg_b, kg_b, sink, conv_w, w_branch, w_out):
    ka, va, kb, vb = kv_heads(p[..., :KV_END], kg_a, kg_b, rope)
    ka_c, va_c, kb_c, vb_c = ctx_kv
    qa = q_heads(p[..., OFF_QA:OFF_QB], qg_a, N_HEADS_A, N_KV_A, rope)
    qb = q_heads(p[..., OFF_QB:OFF_CONV], qg_b, N_HEADS_B, N_KV_B, rope)
    o_a = global_attention(qa, ka, va, ka_c, va_c)
    o_b = window_attention(qb, kb, vb, kb_c, vb_c, sink.reshape(N_KV_B, N_HEADS_B // N_KV_B))
    o_c = short_conv(p[..., OFF_CONV:OFF_GATE], conv_w)
    return merge_branches(o_a, o_b, o_c, p[..., OFF_GATE:], w_branch, w_out)

def context_mixer(pc, ctx_kv, qg_a, qg_b, sink, conv_w, w_branch, w_out):
    B, L, _ = pc.shape
    ka_c, va_c, kb_c, vb_c = ctx_kv
    qa = q_heads(pc[..., OFF_QA:OFF_QB], qg_a, N_HEADS_A, N_KV_A, None)
    qb = q_heads(pc[..., OFF_QB:OFF_CONV], qg_b, N_HEADS_B, N_KV_B, None)
    o_a = attend(qa, ka_c, va_c, None, None).reshape(B, L, -1)
    o_b = attend(qb, kb_c, vb_c, None, sink.reshape(N_KV_B, N_HEADS_B // N_KV_B)).reshape(B, L, -1)
    o_c = short_conv(pc[..., OFF_CONV:OFF_GATE], conv_w)
    return merge_branches(o_a, o_b, o_c, pc[..., OFF_GATE:], w_branch, w_out)

def expert_choice_ffn(h, w_router, w_g, w_u, w_d):
    B, n, D = h.shape
    cap = CAPACITY_FACTOR * n // N_EXPERTS
    logits = jnp.einsum('bnd,de->ben', h, w_router, preferred_element_type=jnp.float32)
    aff = jax.nn.softmax(logits, axis=1)
    gate, idx = lax.top_k(aff, cap)
    bi = jnp.arange(B)[:, None, None]
    xs = h[bi, idx]
    a = jnp.einsum('becd,edf->becf', xs, w_g)
    u = jnp.einsum('becd,edf->becf', xs, w_u)
    y = jnp.einsum('becf,efd->becd', jax.nn.silu(a) * u, w_d)
    return jnp.zeros_like(h).at[bi, idx].add(y * gate[..., None].astype(y.dtype))

def first_inputs(seed: int = 0) -> dict:
    key = jax.random.key(seed)
    ks = jax.random.split(key, 22)
    D = D_MODEL

    def nrm(k, shape, scale):
        return jax.random.normal(k, shape, jnp.float32) * scale

    return {
        "x": nrm(ks[0], (BATCH, SEQ, D), 1.0),
        "c": nrm(ks[1], (BATCH, D), 1.0),
        "ctx": nrm(ks[2], (BATCH, CTX_LEN, D), 1.0),
        "c_ctx": nrm(ks[3], (D,), 1.0),
        "w_ada": nrm(ks[4], (DEPTH, D, 6 * D), 0.5 * D ** -0.5),
        "b_ada": nrm(ks[5], (DEPTH, 6 * D), 0.02),
        "g_mix": 1.0 + nrm(ks[6], (DEPTH, D), 0.02),
        "g_ffn": 1.0 + nrm(ks[7], (DEPTH, D), 0.02),
        "w_in": nrm(ks[8], (DEPTH, D, PROJ_WIDTH), D ** -0.5),
        "qg_a": 1.0 + nrm(ks[9], (DEPTH, HEAD_DIM), 0.02),
        "kg_a": 1.0 + nrm(ks[10], (DEPTH, HEAD_DIM), 0.02),
        "qg_b": 1.0 + nrm(ks[11], (DEPTH, HEAD_DIM), 0.02),
        "kg_b": 1.0 + nrm(ks[12], (DEPTH, HEAD_DIM), 0.02),
        "sink_b": nrm(ks[13], (DEPTH, N_HEADS_B), 0.5),
        "conv_w": nrm(ks[14], (DEPTH, CONV_K, BRANCH_WIDTH), CONV_K ** -0.5),
        "w_branch": nrm(ks[15], (DEPTH, N_BRANCH, BRANCH_WIDTH, D), BRANCH_WIDTH ** -0.5),
        "w_out": nrm(ks[16], (DEPTH, D, D), D ** -0.5),
        "w_router": nrm(ks[17], (DEPTH, D, N_EXPERTS), D ** -0.5),
        "w_e_gate": nrm(ks[18], (DEPTH, N_EXPERTS, D, EXPERT_HIDDEN), D ** -0.5),
        "w_e_up": nrm(ks[19], (DEPTH, N_EXPERTS, D, EXPERT_HIDDEN), D ** -0.5),
        "w_e_down": nrm(ks[20], (DEPTH, N_EXPERTS, EXPERT_HIDDEN, D), EXPERT_HIDDEN ** -0.5),
    }

def first_block(x, c, ctx, c_ctx, w_ada, b_ada, g_mix, g_ffn, w_in, qg_a, kg_a, qg_b, kg_b, sink_b,
              conv_w, w_branch, w_out, w_router, w_e_gate, w_e_up, w_e_down):
    n = x.shape[1]
    rope = rope_tables(n)
    silu_c = jax.nn.silu(c)
    silu_cc = jax.nn.silu(c_ctx)
    xc = ctx
    for l in range(DEPTH):
        last = l == DEPTH - 1
        mod = silu_c @ w_ada[l] + b_ada[l]
        sh1, sc1, gt1, sh2, sc2, gt2 = [m[:, None, :] for m in jnp.split(mod, 6, axis=-1)]
        modc = silu_cc @ w_ada[l] + b_ada[l]
        shc1, scc1, gtc1, shc2, scc2, gtc2 = jnp.split(modc, 6)

        hc = modulate(rmsnorm(xc, g_mix[l]), shc1, scc1)
        pc = hc @ (w_in[l][:, :KV_END] if last else w_in[l])
        ctx_kv = kv_heads(pc[..., :KV_END], kg_a[l], kg_b[l], None)

        h = modulate(rmsnorm(x, g_mix[l]), sh1, sc1)
        p = h @ w_in[l]
        x = x + gt1 * latent_mixer(p, ctx_kv, rope, qg_a[l], kg_a[l], qg_b[l], kg_b[l], sink_b[l],
                                   conv_w[l], w_branch[l], w_out[l])
        h2 = modulate(rmsnorm(x, g_ffn[l]), sh2, sc2)
        x = x + gt2 * expert_choice_ffn(h2, w_router[l], w_e_gate[l], w_e_up[l], w_e_down[l])

        if not last:
            xc = xc + gtc1 * context_mixer(pc, ctx_kv, qg_a[l], qg_b[l], sink_b[l], conv_w[l],
                                           w_branch[l], w_out[l])
            hc2 = modulate(rmsnorm(xc, g_ffn[l]), shc2, scc2)
            xc = xc + gtc2 * expert_choice_ffn(hc2, w_router[l], w_e_gate[l], w_e_up[l], w_e_down[l])
    return x


DEPTH_2 = 1

A_HEADS = D_MODEL // (2 * HEAD_DIM)
A_KV_HEADS = max(1, A_HEADS // 4)
A_WINDOW = 128
B_HEADS = D_MODEL // (2 * HEAD_DIM)
B_PATTERNS = ((128, 1), (512, 4), (2048, 16))
BLOCK = 128
ROPE_THETA = 10000.0
NEG = -1e30

A_WIDTH = A_HEADS * HEAD_DIM
A_KV_WIDTH = A_KV_HEADS * HEAD_DIM
B_WIDTH = B_HEADS * HEAD_DIM
MIX_WIDTH = A_WIDTH + B_WIDTH
IN_SPLITS = (A_WIDTH, A_KV_WIDTH, A_KV_WIDTH, A_WIDTH, B_WIDTH, B_WIDTH, B_WIDTH, B_WIDTH)
IN_WIDTH = sum(IN_SPLITS)


def rmsnorm_2(t, gain):
    tf = t.astype(jnp.float32)
    tf = tf * lax.rsqrt(jnp.mean(tf * tf, axis=-1, keepdims=True) + EPS)
    return (tf * gain.astype(jnp.float32)).astype(t.dtype)

def rope(t, pos):
    half = HEAD_DIM // 2
    inv = ROPE_THETA ** (-jnp.arange(half, dtype=jnp.float32) / half)
    ang = pos.astype(jnp.float32)[:, None] * inv[None, :]
    cos = jnp.cos(ang)[:, None, :]
    sin = jnp.sin(ang)[:, None, :]
    tf = t.astype(jnp.float32)
    t1, t2 = tf[..., :half], tf[..., half:]
    return jnp.concatenate([t1 * cos - t2 * sin, t2 * cos + t1 * sin], axis=-1).astype(t.dtype)

def banded_attention(q, k, v, max_dist, sinks=None):
    n, L, h, d = q.shape
    hkv = k.shape[2]
    g = h // hkv
    nb = -(-L // BLOCK)
    lp = nb * BLOCK
    pad = lp - L
    q = jnp.pad(q, ((0, 0), (0, pad), (0, 0), (0, 0)))
    k = jnp.pad(k, ((0, 0), (BLOCK, pad), (0, 0), (0, 0)))
    v = jnp.pad(v, ((0, 0), (BLOCK, pad), (0, 0), (0, 0)))
    qb = q.reshape(n, nb, BLOCK, hkv, g, d)
    kb = k.reshape(n, nb + 1, BLOCK, hkv, d)
    vb = v.reshape(n, nb + 1, BLOCK, hkv, d)
    kw = jnp.concatenate([kb[:, :-1], kb[:, 1:]], axis=2)
    vw = jnp.concatenate([vb[:, :-1], vb[:, 1:]], axis=2)
    s = jnp.einsum("nbqkgd,nbskd->nbkgqs", qb, kw,
                   preferred_element_type=jnp.float32) * (d ** -0.5)
    qi = jnp.arange(BLOCK)[:, None]
    sj = jnp.arange(2 * BLOCK)[None, :]
    dist = qi - sj + BLOCK
    key_pos = jnp.arange(nb)[:, None] * BLOCK - BLOCK + sj
    valid = ((dist >= 0) & (dist <= max_dist))[None] & (key_pos >= 0)[:, None, :]
    s = jnp.where(valid[None, :, None, None], s, NEG)
    m = s.max(axis=-1)
    if sinks is not None:
        sk = sinks.astype(jnp.float32).reshape(hkv, g)[None, None, :, :, None]
        m = jnp.maximum(m, sk)
    p = jnp.exp(s - m[..., None])
    l = p.sum(axis=-1)
    if sinks is not None:
        l = l + jnp.exp(sk - m)
    o = jnp.einsum("nbkgqs,nbskd->nbqkgd", p, vw.astype(jnp.float32))
    m = m.transpose(0, 1, 4, 2, 3)
    l = l.transpose(0, 1, 4, 2, 3)
    o = o / l[..., None]
    o = o.reshape(n, lp, h, d)[:, :L]
    m = m.reshape(n, lp, h)[:, :L]
    l = l.reshape(n, lp, h)[:, :L]
    return o, m, l

def dilated_attention(q, k, v):
    b, S, h, d = q.shape
    outs, ms, ls = [], [], []
    for window, dil in B_PATTERNS:
        L = S // dil

        def fold(t):
            return t.reshape(b, L, dil, h, d).transpose(0, 2, 1, 3, 4).reshape(b * dil, L, h, d)

        o, m, l = banded_attention(fold(q), fold(k), fold(v), window // dil)
        outs.append(o.reshape(b, dil, L, h, d).transpose(0, 2, 1, 3, 4).reshape(b, S, h, d))
        ms.append(m.reshape(b, dil, L, h).transpose(0, 2, 1, 3).reshape(b, S, h))
        ls.append(l.reshape(b, dil, L, h).transpose(0, 2, 1, 3).reshape(b, S, h))
    o = jnp.stack(outs)
    m = jnp.stack(ms)
    l = jnp.stack(ls)
    w = l * jnp.exp(m - m.max(axis=0, keepdims=True))
    return (w[..., None] * o).sum(axis=0) / w.sum(axis=0)[..., None]

def second_inputs(seed: int = 0) -> dict:
    key = jax.random.key(seed)
    ks = jax.random.split(key, 10)
    f32 = jnp.float32
    x = jax.random.normal(ks[0], (BATCH, SEQ, D_MODEL), f32)
    norm_gain = 1.0 + 0.1 * jax.random.normal(ks[1], (DEPTH_2, D_MODEL), f32)
    w_in = jax.random.normal(ks[2], (DEPTH_2, D_MODEL, IN_WIDTH), f32) * D_MODEL ** -0.5
    q_norm_a = 1.0 + 0.1 * jax.random.normal(ks[3], (DEPTH_2, HEAD_DIM), f32)
    k_norm_a = 1.0 + 0.1 * jax.random.normal(ks[4], (DEPTH_2, HEAD_DIM), f32)
    sinks_a = 0.5 * jax.random.normal(ks[5], (DEPTH_2, A_HEADS), f32)
    q_norm_b = 1.0 + 0.1 * jax.random.normal(ks[6], (DEPTH_2, HEAD_DIM), f32)
    k_norm_b = 1.0 + 0.1 * jax.random.normal(ks[7], (DEPTH_2, HEAD_DIM), f32)
    w_out = jax.random.normal(ks[8], (DEPTH_2, MIX_WIDTH, D_MODEL), f32) * MIX_WIDTH ** -0.5
    return {"x": x, "norm_gain": norm_gain, "w_in": w_in,
            "q_norm_a": q_norm_a, "k_norm_a": k_norm_a, "sinks_a": sinks_a,
            "q_norm_b": q_norm_b, "k_norm_b": k_norm_b, "w_out": w_out}

def second_block(x, norm_gain, w_in, q_norm_a, k_norm_a, sinks_a, q_norm_b, k_norm_b, w_out):
    b, S, _ = x.shape
    pos = jnp.arange(S)
    split_at = [int(c) for c in np.cumsum(IN_SPLITS)[:-1]]
    for i in range(DEPTH_2):
        hdn = rmsnorm_2(x, norm_gain[i])
        proj = jnp.einsum("bsd,de->bse", hdn, w_in[i])
        q_a, k_a, v_a, g_a, q_b, k_b, v_b, g_b = jnp.split(proj, split_at, axis=-1)

        q_a = rope(rmsnorm_2(q_a.reshape(b, S, A_HEADS, HEAD_DIM), q_norm_a[i]), pos)
        k_a = rope(rmsnorm_2(k_a.reshape(b, S, A_KV_HEADS, HEAD_DIM), k_norm_a[i]), pos)
        v_a = v_a.reshape(b, S, A_KV_HEADS, HEAD_DIM)
        o_a, _, _ = banded_attention(q_a, k_a, v_a, A_WINDOW - 1, sinks=sinks_a[i])
        o_a = o_a.reshape(b, S, A_WIDTH).astype(x.dtype) * jax.nn.silu(g_a)

        q_b = rope(rmsnorm_2(q_b.reshape(b, S, B_HEADS, HEAD_DIM), q_norm_b[i]), pos)
        k_b = rope(rmsnorm_2(k_b.reshape(b, S, B_HEADS, HEAD_DIM), k_norm_b[i]), pos)
        v_b = v_b.reshape(b, S, B_HEADS, HEAD_DIM)
        o_b = dilated_attention(q_b, k_b, v_b)
        o_b = o_b.reshape(b, S, B_WIDTH).astype(x.dtype) * jax.nn.silu(g_b)

        mixed = jnp.concatenate([o_a, o_b], axis=-1)
        x = x + jnp.einsum("bse,ed->bsd", mixed, w_out[i])
    return x


def setup_inputs(seed=0):
    out = dict(first_inputs(seed))
    for name, value in second_inputs(seed + 1).items():
        if name != "x":
            out[name + "_2"] = value
    return out


def reference(
    x, c, ctx, c_ctx, w_ada, b_ada, g_mix, g_ffn, w_in, qg_a, kg_a, qg_b, kg_b, sink_b, conv_w,
    w_branch, w_out, w_router, w_e_gate, w_e_up, w_e_down, norm_gain_2, w_in_2, q_norm_a_2,
    k_norm_a_2, sinks_a_2, q_norm_b_2, k_norm_b_2, w_out_2,
):
    x = first_block(
        x, c, ctx, c_ctx, w_ada, b_ada, g_mix, g_ffn, w_in, qg_a, kg_a, qg_b, kg_b, sink_b,
        conv_w, w_branch, w_out, w_router, w_e_gate, w_e_up, w_e_down,
    )
    return second_block(
        x, norm_gain_2, w_in_2, q_norm_a_2, k_norm_a_2, sinks_a_2, q_norm_b_2, k_norm_b_2,
        w_out_2,
    )


_drawn_inputs = setup_inputs


def setup_inputs(seed=0):
    import zlib

    import numpy as np

    out = dict(_drawn_inputs(seed))
    spreads = {}
    factors = {'ctx': 3.119,
     'g_mix': 4.549,
     'g_ffn': 5.887,
     'qg_a': 8.0,
     'kg_a': 8.0,
     'qg_b': 8.0,
     'kg_b': 8.0,
     'sink_b': 8.0,
     'norm_gain_2': 2.706,
     'q_norm_a_2': 8.0,
     'k_norm_a_2': 8.0,
     'sinks_a_2': 8.0,
     'q_norm_b_2': 8.0,
     'k_norm_b_2': 8.0}
    for name, (base, spread) in spreads.items():
        noise = np.random.default_rng([zlib.crc32(name.encode()), seed]).standard_normal(out[name].shape)
        drawn = base * np.exp(spread * noise) if base else spread * noise
        out[name] = __import__('jax').numpy.asarray(drawn.astype(out[name].dtype))
    for name, factor in factors.items():
        out[name] = (out[name] * factor).astype(out[name].dtype)
    return out
```

```python
from contextlib import ExitStack

import numpy as np

import concourse.bass as bass
from concourse import mybir

F32 = mybir.dt.float32
ALU = mybir.AluOpType
ACT = mybir.ActivationFunctionType
AX = mybir.AxisListType

P = 128
D = 1024
KD = D // P
NX, NC = 512, 256
NT = NX + NC
DEPTH = 2
HD = 64
HEADS = 8
EPS = 1e-6
E = 16
FH = 1024
CX, CC = 2 * NX // E, 2 * NC // E
SCALE = HD ** -0.5
NEG = -1e30

CH = 256
RING = 6

KV_END, OFF_QA, OFF_QB, OFF_CONV, OFF_GATE = 512, 512, 1024, 1536, 3072
Q2A, K2A, G2A, Q2B, K2B, V2B, G2B, W2 = 0, 512, 768, 1280, 1792, 2304, 2816, 3328

PB_ADA, PG_MIX, PG_FFN, PCONV, PQK, PEXTRA = 0, 48, 56, 64, 76, 80
SH1, SC1, GT1, SH2, SC2, GT2 = (8 * j for j in range(6))

C_ID, C_ROT, C_HEAD, C_MASK, C_IOTA, C_COS, C_SIN, C_COS2, C_SIN2, C_END = (
    0, 128, 256, 384, 384 + 8 * P, 384 + 8 * P + CX, 384 + 8 * P + CX + NX,
    384 + 8 * P + CX + 2 * NX, 384 + 8 * P + CX + 3 * NX, 384 + 8 * P + CX + 4 * NX)
PROWS = (96, 92)
M_DIL, M_BAND, M_PREV, M_NEXT = 0, 4 * P, 6 * P, 7 * P


def constants():
    c = np.zeros((P, C_END), np.float32)
    c[:, C_ID:C_ID + P] = np.eye(P)
    for f in range(P):
        h, r = f // HD * HD, f % HD
        if r < HD // 2:
            c[h + r + HD // 2, C_ROT + f] = -1.0
        else:
            c[h + r - HD // 2, C_ROT + f] = 1.0
        c[h:h + HD, C_HEAD + f] = 1.0
    q, k = np.arange(P)[:, None], np.arange(P)[None, :]
    for n, b in enumerate((2, 2, 1, 0)):
        dist = P * b + q - k
        count = ((dist >= 0) & (dist <= 128)) * 1 + ((dist >= 0) & (dist % 4 == 0)) + ((dist >= 0) & (dist % 16 == 0))
        c[:, C_MASK + M_DIL + n * P:C_MASK + M_DIL + (n + 1) * P] = np.where(
            count > 0, np.log(np.maximum(count, 1)) / SCALE, NEG)
    c[:, C_MASK + M_BAND:C_MASK + M_BAND + P] = np.where(k > q, 0, NEG)
    c[:, C_MASK + M_BAND + P:C_MASK + M_BAND + 2 * P] = np.where(k <= q, 0, NEG)
    c[:, C_MASK + M_PREV:C_MASK + M_PREV + P] = np.where(k >= q, 0, NEG)
    c[:, C_MASK + M_NEXT:C_MASK + M_NEXT + P] = np.where(k <= q, 0, NEG)
    c[:, C_IOTA:C_IOTA + CX] = np.arange(CX)
    n4 = HD // 4
    inv = np.float32(10000.0) ** (-np.arange(n4, dtype=np.float32) / np.float32(n4))
    t = np.arange(NX)
    ang = np.concatenate([(t // 64).astype(np.float32)[:, None] * inv, (t % 64).astype(np.float32)[:, None] * inv], 1)
    n2 = HD // 2
    inv2 = np.float32(10000.0) ** (-np.arange(n2, dtype=np.float32) / np.float32(n2))
    ang2 = t.astype(np.float32)[:, None] * inv2
    for f in range(P):
        c[f, C_COS:C_COS + NX] = np.cos(ang[:, f % n2])
        c[f, C_SIN:C_SIN + NX] = np.sin(ang[:, f % n2])
        c[f, C_COS2:C_COS2 + NX] = np.cos(ang2[:, f % n2])
        c[f, C_SIN2:C_SIN2 + NX] = np.sin(ang2[:, f % n2])
    return c


class Count:

    def __init__(self, sem, keys):
        self.sem, self.at = sem, {k: n + 1 for n, k in enumerate(keys)}
        assert len(self.at) == len(keys)


def program(nc, x, c, ctx_in, c_ctx, w_ada, b_ada, g_mix, g_ffn, w_in, qg_a, kg_a, qg_b, kg_b, sink_b, conv_w,
            w_branch, w_out, w_router, w_e_gate, w_e_up, w_e_down, norm_gain_2, w_in_2, q_norm_a_2, k_norm_a_2,
            sinks_a_2, q_norm_b_2, k_norm_b_2, w_out_2, consts, out):
    with ExitStack() as stack:
        def sb(name, shape):
            return stack.enter_context(nc.sbuf_tensor(name, shape, F32))

        def sem(name):
            return stack.enter_context(nc.semaphore(name))

        ps = stack.enter_context(nc.psum_tensor("ps", [P, 8 * 512], F32))
        ring = sb("ring", [P, RING, 8 * CH])
        xT = sb("xT", [P, KD, NT])
        hT = sb("hT", [P, KD * NT])
        merged = sb("merged", [P, KD * NT])
        qbuf = sb("qbuf", [P, 4 * NT])
        obuf = sb("obuf", [P, 8 * NT])
        kbuf = sb("kbuf", [P, 2 * NT])
        vbuf = sb("vbuf", [P, 2560])
        con = sb("con", [P, C_COS2])
        ones = sb("ones", [P, P])
        pv = sb("pv", [P, DEPTH, 96])
        mod = sb("mod", [P, 48 * 2])
        amp = sb("amp", [P, 2, KD * 2])
        epsn = sb("epsn", [P, 2])
        zero2 = sb("zero2", [P, KD * 2])
        silc = sb("silc", [P, 2 * KD])
        tmpc = sb("tmpc", [P, 2 * KD])
        sinks = sb("sinks", [P, 3, HEADS])
        nsink = sb("nsink", [P, 3, HEADS])
        wr = sb("wr", [P, KD, E])
        sq = sb("sq", [P, NT])
        rs = sb("rs", [P, NT])
        prob = sb("prob", [P, 2, NT])
        probT = sb("probT", [P, 2, NT])
        mxn = sb("mxn", [P, HEADS])
        nms = sb("nms", [P, 2, HEADS])
        lsum = sb("lsum", [P, 2, HEADS])
        sdif = sb("sdif", [P, HEADS])
        sexp = sb("sexp", [P, HEADS])
        route = sb("route", [P, 12 * E + 2])

        ident = con[:, C_ID:C_ID + P]
        h3 = hT[:].rearrange("p (k t) -> p k t", k=KD)
        m3 = merged[:].rearrange("p (k t) -> p k t", k=KD)
        tok = merged[:].rearrange("p (t d) -> p t d", t=6)
        q3 = qbuf[:].rearrange("p (k t) -> p k t", k=4)
        o4 = obuf[:].rearrange("p (b k t) -> p b k t", b=2, k=4)
        k3 = kbuf[:].rearrange("p (k t) -> p k t", k=2)
        v4 = vbuf[:, 0:2 * 6 * P].rearrange("p (b t f) -> p b t f", b=2, t=6)
        mod3 = mod[:].rearrange("p (k w) -> p k w", w=2)
        amp4 = amp[:].rearrange("p n (k w) -> p n k w", w=2)
        zero3 = zero2[:].rearrange("p (k w) -> p k w", w=2)
        q2a = qbuf[:, 0:4 * NX].rearrange("p (k t) -> p k t", k=4)
        q2b = merged[:, 8 * NX:12 * NX].rearrange("p (k t) -> p k t", k=4)
        sg2 = merged[:, 0:8 * NX].rearrange("p (k t) -> p k t", k=8)
        o2 = obuf[:, 0:8 * NX].rearrange("p (k t) -> p k t", k=8)
        k2b = obuf[:, 8 * NX:12 * NX].rearrange("p (k t) -> p k t", k=4)
        k2a = kbuf[:, 0:NX].rearrange("p (k t) -> p k t", k=1)
        v2 = vbuf[:].rearrange("p (t f) -> p t f", t=4)
        xs4 = hT[:, 0:8 * 192].rearrange("p (k e c) -> p k e c", k=8, e=2)
        hm2 = hT[:, 1536:1536 + 2 * 768].rearrange("p (e f) -> p e f", e=2)
        eg2 = hT[:, 3072:3072 + 2 * 768].rearrange("p (e f) -> p e f", e=2)
        yx, yc = qbuf[:, 0:D], qbuf[:, D:2 * D]
        selx = obuf[:, 0:512].rearrange("p (t c) -> p t c", t=4)
        gselx = obuf[:, 512:1024].rearrange("p (t c) -> p t c", t=4)
        selc = obuf[:, 1024:1024 + 4 * CC].rearrange("p (t c) -> p t c", t=2)
        gselc = obuf[:, 1152:1152 + 4 * CC].rearrange("p (t c) -> p t c", t=2)
        gTx, gTc = obuf[:, 1536:1536 + NX], obuf[:, 2048:2048 + NC]
        gates3 = route[:, 6 * E:12 * E].rearrange("p (t e) -> p t e", t=6)
        work = prob[0:E, 1, :]
        selm = probT[0:E, 0, :]
        slotm = probT[0:E, 1, :]
        rone = sq[0:E, :]
        m8 = sexp[0:E, :]

        s_const, s_param, s_x, s_rope2, s_router, s_out = (sem(n) for n in (
            "const_loaded", "param_loaded", "x_loaded", "rope2_loaded", "router_loaded", "out_stored"))
        w_full = [sem(f"weights_landed{i}") for i in range(RING)]
        full = [sem(f"psum_full{i}") for i in range(5)]
        free = [sem(f"psum_free{i}") for i in range(5)]
        act_step, dve_step, pool_step = sem("act_step"), sem("dve_step"), sem("pool_step")
        s_phase = sem("phase_done")
        slot_free = sem("slot_found_free")
        pv_ready = sem("param_turned")
        BANK = [0, 1024, 2048, 3072, 3584]

        def units_first(l, br):
            units = []
            streams = [("x", i) for i in range(NX // P)] + ([("c", i) for i in range(NC // P)] if l == 0 else [])
            for st, i in streams:
                q0 = i * P if st == "x" else NX + i * P
                for h in range(HEADS):
                    j, half = h % 4, h // 4
                    if st == "c":
                        segs, masks, lo, hi = [(512, NC, NX)], [], 512, 768
                        tiles = {512: 4, 640: 5}
                    elif br == 0:
                        segs, masks, lo, hi = [(0, NX, 0), (512, NC, NX)], [], 0, 768
                        tiles = {n * P: n for n in range(6)}
                    else:
                        a, b = max(0, i - 1), min(NX // P - 1, i + 1)
                        n = (b - a + 1) * P
                        lo, hi = 512 - n, 768
                        segs = [(lo, n, a * P), (512, NC, NX)]
                        masks = ([(lo, P, M_PREV)] if a < i else []) + ([(512 - P, P, M_NEXT)] if b > i else [])
                        tiles = {lo + n * P: a + n for n in range(b - a + 1)} | {512: 4, 640: 5}
                    units.append(dict(q0=q0, h=h, qt=q0 // P, j=j, half=half, kj=br, segs=segs, masks=masks, lo=lo,
                                      hi=hi, tiles=sorted(tiles.items()), vcol=half * HD))
            return units

        def units_second(br):
            units = []
            for i in range(NX // P):
                for h in range(HEADS):
                    if br == 0:
                        j, half, kj, vcol = h % 4, h // 4, 0, (h // 4) * HD
                        a = max(0, i - 1)
                        n = (i - a + 1) * P
                        masks = [(0, n, M_BAND + 2 * P - n)]
                    else:
                        j, half, kj, vcol = h // 2, h % 2, h // 2, P + h * HD
                        a, n = 0, (i + 1) * P
                        masks = [(0, n, M_DIL + 4 * P - n)]
                    units.append(dict(q0=i * P, h=h, qt=i, j=j, half=half, kj=kj, segs=[(0, n, a * P)], masks=masks,
                                      lo=0, hi=n, tiles=[(m * P, a + m) for m in range(n // P)], vcol=vcol))
            return units

        UNITS = {(l, br): units_first(l, br) for l in range(DEPTH) for br in range(2)}
        UNITS |= {(2, br): units_second(br) for br in range(2)}

        def attention_order(key):
            n = len(UNITS[key])
            order = []
            for s in range(n + 3):
                if s < n:
                    order.append(("S", key, s))
                if 0 <= s - 1 < n:
                    order.append(("T", key, s - 1))
                if 0 <= s - 2 < n:
                    order.append(("V", key, s - 2))
                if s >= 3 and (s - 3) % HEADS == HEADS - 1:
                    order.append(("O", key, (s - 3) // HEADS))
            return order

        def pipelined(jobs):
            order, sums, rots = [], [], []
            for j in jobs:
                order.append(j)
                if rots:
                    order.append(rots.pop(0))
                if sums:
                    t = sums.pop(0)
                    order.append(("hs",) + t)
                    rots.append(("rot",) + t)
                if j[0] == "qk":
                    sums.append(j[1:])
            order += rots
            for t in sums:
                order += [("hs",) + t, ("rot",) + t]
            return order

        def plan_layer(l):
            first = [("qk", l, "ka"), ("v", l, 0), ("qk", l, "kb"), ("v", l, 1)]
            first += [("qk", l, f"qa{j}") for j in range(4)]
            first += [(f"conv_{w}", l, m) for hf in range(2) for w in "cxb" for m in (2 * hf, 2 * hf + 1)]
            gates = {br: [(w, l, br, d) for d in range(KD) for w in ("gate", "branch")] for br in range(3)}
            order = pipelined(first) + attention_order((l, 0))
            order += pipelined([("qk", l, f"qb{j}") for j in range(4)] + gates[2])
            order += attention_order((l, 1)) + gates[0] + gates[1]
            order += [("wout", l, d) for d in range(KD)]
            return order

        def plan_second():
            first = [("qk", 2, "ka"), ("v", 2, 0)] + [("qk", 2, f"qa{j}") for j in range(4)]
            first += [("qk", 2, f"kb{j}") for j in range(4)] + [("qk", 2, f"qb{j}") for j in range(4)]
            first += [("v", 2, 1), ("v", 2, 2)] + [("silg", 2, d) for d in range(8)]
            return (pipelined(first) + attention_order((2, 0)) + attention_order((2, 1))
                    + [("wout", 2, d) for d in range(KD)])

        PLAN = {0: plan_layer(0), 1: plan_layer(1), 2: plan_second()}
        PH = [(0, "mix"), (0, "ffn"), (1, "mix"), (1, "ffn"), (2, "mix")]
        every = [j for n in range(3) for j in PLAN[n]]

        def of(*kinds):
            return [j for j in every if j[0] in kinds]

        def event(name, keys):
            return Count(sem(name), keys)

        sq_ready = event("square_ready", [("n",) + ph + (d,) for ph in PH for d in range(KD)])
        hpre = event("h_scaled", [ph + (d,) for ph in PH for d in range(KD)])
        h_ready = event("h_ready", [ph + (d,) for ph in PH for d in range(KD)])
        hs_of = {n: [j for j in PLAN[n] if j[0] == "hs"] for n in range(3)}
        rms_ready = event("root_ready", [("norm", 0, "mix")] + hs_of[0] + [("norm", 0, "ffn"), ("norm", 1, "mix")] + hs_of[1]
                          + [("norm", 1, "ffn"), ("norm", 2, "mix")] + hs_of[2])
        qsq_ready = event("head_square_ready", of("qk"))
        qn_ready = event("head_normed", of("hs"))
        q_ready = event("head_rotated", of("rot"))
        v_ready = event("values_ready", of("v"))
        cg_ready = event("conv_gate_copied", of("conv_c"))
        cu_used = event("conv_input_used", of("conv_x"))
        oc_ready = event("conv_ready", of("conv_b"))
        nm_ready = event("row_max_ready", of("S"))
        p_ready = event("exp_ready", of("S"))
        pt_ready = [event(f"expT_ready{r}", [j for j in of("T") if j[2] % 2 == r]) for r in range(2)]
        pv_done = event("values_summed", of("V"))
        o_read = event("out_normalised", of("O"))
        oT_ready = event("outT_ready", of("O"))
        with_sink = [j for j in of("O") if j[1] in ((0, 1), (1, 1), (2, 0))]
        sd_ready = event("sink_shifted", with_sink)
        se_ready = event("sink_exp", with_sink)
        sig_ready = event("gate_sigmoid", of("gate", "silg"))
        gate_used = event("gate_used", of("branch", "silg"))
        ada_done = event("modulation_ready", [0, 1])
        sil_sig = sem("cond_sigmoid")
        sil_ready = sem("cond_ready")
        aff_max, aff_exp = event("router_max", [0, 1]), event("router_exp", [0, 1])
        aff_ready = event("router_softmax", [0, 1])
        slots_ready = event("slots_ready", [0, 1])
        route_ready = event("route_ready", [0, 1])
        tok_ready = event("tok_ready", [0, 1])
        sel_ready, gT_ready, xs_ready = sem("selection_ready"), sem("gatesT_ready"), sem("expert_in_ready")
        eg_sig, hm_ready, y_ready = sem("expert_gate_sigmoid"), sem("expert_hidden"), sem("expert_out_copied")
        out_copied = event("out_copied", list(range(NX // P)))

        PAIRS = E // 2

        job = {}
        used, parts = [0] * 5, [0] * 5
        turn = [0]

        def loop_plan(l):
            js = [("gx", 1)] + ([("gc", 1)] if l == 0 else []) + [("gt", 1)]
            js += [("eg0", 4), ("eu0", 4), ("eg1", 4), ("eu1", 4), ("ed0", 4), ("ed1", 4)]
            return js + [(f"sc{d}", 1) for d in range(KD)]

        loop_job = {}

        def open_loop(l):
            js = [(k, n, i % 3) for i, (k, n) in enumerate(loop_plan(l))]
            per_job = [sum(1 for _, _, s in js if s == t) for t in range(3)]
            per_part = [sum(n for _, n, s in js if s == t) for t in range(3)]
            u, f = list(used), list(parts)
            for k, n, s in js:
                f[s] += n
                loop_job[l, k] = (s, u[s], per_job[s], f[s], per_part[s])
                u[s] += 1
            for t in range(3):
                used[t] += PAIRS * per_job[t]
                parts[t] += PAIRS * per_part[t]

        chunks = []
        landed = [0] * RING
        chunk_at = []
        chunk_end = []
        chunk_key = {}

        def add_chunk(key, dmas):
            n = len(chunks)
            s = n % RING
            landed[s] += 16 * len(dmas)
            chunks.append(dmas)
            chunk_at.append((s, landed[s]))
            chunk_end.append(None)
            chunk_key[key] = n

        def cols(w, lo, n):
            return w[:, lo:lo + n].rearrange("(k p) f -> p k f", p=P)

        def ring3(s, k=8):
            return ring[:, s, :].rearrange("p (k f) -> p k f", k=k)

        def plain(w, lo):
            return [((slice(None), 8, slice(0, CH)), cols(w, lo, CH))]

        def paired(w, lo, jj):
            hs = [2 * jj, 4 + 2 * jj, 2 * jj + 1, 5 + 2 * jj]
            return [((slice(None), 8, slice(n * HD, (n + 1) * HD)), cols(w, lo + h * HD, HD)) for n, h in enumerate(hs)]

        ROUND = [(w, e, n) for e in range(2) for w in ("eg", "eu") for n in range(4)]
        ROUND += [("ed", e, n) for e in range(2) for n in range(4)]
        EXPERT_W = {"eg": w_e_gate, "eu": w_e_up, "ed": w_e_down}

        def layer_chunks(l):
            wi, wb, wo = w_in[l], w_branch[l], w_out[l]
            for n in range(24):
                add_chunk(("ada", l, n), plain(w_ada[l], n * CH))
            for n in range(2):
                add_chunk(("kv", l, n), plain(wi, n * CH))
            for jj in range(2):
                add_chunk(("qa", l, jj), paired(wi, OFF_QA, jj))
            for hf in range(2):
                for w, off in (("c", 512), ("x", 1024), ("b", 0)):
                    add_chunk(("conv_" + w, l, hf), plain(wi, OFF_CONV + off + hf * CH))
            for jj in range(2):
                add_chunk(("qb", l, jj), paired(wi, OFF_QB, jj))
            for br in (2, 0, 1):
                for hf in range(2):
                    add_chunk(("branch", l, br, hf), [((slice(None), 4, slice(0, 512)), cols(wb[br], hf * 512, 512))])
                    for n in (2 * hf, 2 * hf + 1):
                        add_chunk(("gate", l, br, n), plain(wi, OFF_GATE + br * D + n * CH))
            for n in range(4):
                add_chunk(("wout", l, n), plain(wo, n * CH))
            LOOPC[l] = len(chunks)
            for i in range(PAIRS):
                for n, (w, e, part) in enumerate(ROUND):
                    add_chunk(("expert", l, i, n), plain(EXPERT_W[w][l, 2 * i + e], part * CH))

        LOOPC = {}
        layer_chunks(0)
        layer_chunks(1)
        for n in range(1):
            add_chunk(("k2a", n), plain(w_in_2[0], K2A))
        for jj in range(2):
            add_chunk(("q2a", jj), paired(w_in_2[0], Q2A, jj))
        for name, off in (("k2b", K2B), ("q2b", Q2B), ("v2b", V2B), ("g2a", G2A), ("g2b", G2B)):
            for n in range(2):
                add_chunk((name, n), plain(w_in_2[0], off + n * CH))
        for n in range(4):
            add_chunk(("wout2", n), plain(w_out_2[0], n * CH))

        block = stack.enter_context(nc.Block())

        def width(l, name):
            return NT if l == 0 or (l == 1 and name in ("ka", "kb")) else NX

        def halves(w):
            return [(0, 512)] + ([(512, w)] if w > 512 else [])

        def qk_dest(l, name):
            if l < 2:
                return {"ka": k3[:, 0, :], "kb": k3[:, 1, :]}.get(name) if name[0] == "k" else q3[:, int(name[2]), :]
            return {"ka": k2a, "qa": q2a, "kb": k2b, "qb": q2b}[name[:2]][:, int(name[2:] or 0), :]

        def gain_col(l, name):
            n = ("qa", "ka", "qb", "kb").index(name[:2])
            return pv[:, l, PQK + n:PQK + n + 1] if l < 2 else pv[:, 1, PEXTRA + 8 + n:PEXTRA + 9 + n]

        def attn_bufs(key):
            l, br = key
            if l < 2:
                return q3, k3, lambda t, c0: v4[:, br, t, c0:c0 + HD]
            return (q2a, q2b)[br], (k2a, k2b)[br], lambda t, c0: v2[:, t, c0:c0 + HD]

        SEL = {0: 4, 1: 2}
        sel_base = {0: 0, 1: SEL[0] * (PAIRS + 1)}
        act_base, dve_base = {}, {}
        PARAM_DMAS = 2 * (3 + 1 + 8 + 1) + 3 + 8 + 1

        def last_rot(key):
            return ("rot", key[0], "qb3" if key[1] else "qa3")

        def last_v(key):
            return ("v", key[0], 2 if key == (2, 1) else key[1])

        o_number = {j[1:]: n for n, j in enumerate(of("O"))}
        SINK = {(0, 1): 0, (1, 1): 1, (2, 0): 2}

        @block.tensor
        def _(pe):
            phases = [0]

            def meet():
                phases[0] += 1
                pe.sem_inc(s_phase, 1)
                pe.wait_ge(s_phase, 4 * phases[0])

            def begin(key, slot=None):
                if slot is None:
                    slot, turn[0] = turn[0], (turn[0] + 1) % 3
                n = used[slot]
                used[slot] += 1
                job[key] = [slot, n, None]
                if n:
                    pe.wait_ge(free[slot], n)
                return BANK[slot]

            def part(mm, key):
                slot = job[key][0]
                parts[slot] += 1
                mm.then_inc(full[slot], 1)
                job[key][2] = parts[slot]

            def weights(key):
                n = chunk_key[key]
                slot, value = chunk_at[n]
                pe.wait_ge(w_full[slot], value)
                return n, slot

            def need(ev, key):
                pe.wait_ge(ev.sem, ev.at[key])

            def norm_sum(ph, w):
                key = ("norm",) + ph
                b = begin(key)
                for d in range(KD):
                    need(sq_ready, ("n",) + ph + (d,))
                    for a, e in halves(w):
                        mm = pe.matmul(ps[:, b + a:b + e], ones[:, :], m3[:, d, a:e], start=d == 0, stop=d == KD - 1)
                part(mm, key)

            def modulation(l):
                if l == 0:
                    pe.wait_ge(sil_ready, 1)
                key = ("ada", l)
                b = begin(key)
                for n in range(24):
                    cn, slot = weights(("ada", l, n))
                    w = ring3(slot)
                    for t in (2 * n, 2 * n + 1):
                        for k in range(KD):
                            mm = pe.matmul(ps[:, b + 2 * t:b + 2 * t + 2], w[:, k, (t % 2) * P:(t % 2 + 1) * P],
                                           silc[:, k:k + KD + 1:KD], start=k == 0, stop=k == KD - 1)
                    part(mm, key)
                    chunk_end[cn] = (job[key][0], job[key][2])

            seen_h = set()

            def product(key, ph, lhs, rhs, w, nk):
                b = begin(key)
                for a, e in halves(w):
                    for k in range(nk):
                        if ph is not None and (ph, k) not in seen_h:
                            need(h_ready, ph + (k,))
                            seen_h.add((ph, k))
                        mm = pe.matmul(ps[:, b + a:b + e], lhs[:, k, :], rhs[:, k, a:e], start=k == 0, stop=k == nk - 1)
                part(mm, key)

            def chunk_of(j):
                kind, l, t = j[0], j[1], j[2]
                if kind == "qk":
                    n = int(t[2:] or 0)
                    if t[0] == "k" and l < 2:
                        return ("kv", l, "ab".index(t[1])), 0
                    if l < 2:
                        return (t[:2], l, n // 2), n % 2
                    return ("k2a", 0) if t == "ka" else ({"qa": "q2a", "kb": "k2b", "qb": "q2b"}[t[:2]], n // 2), n % 2
                if kind == "v":
                    return ((("kv", l, t), 1) if l < 2 else (("k2a", 0), 1) if t == 0 else (("v2b", t - 1), 0))
                if kind[:4] == "conv":
                    return (kind, l, t // 2), t % 2
                if kind == "gate":
                    return ("gate", l, t, j[3] // 2), j[3] % 2
                if kind == "branch":
                    return ("branch", l, t, j[3] // 4), j[3] % 4
                if kind == "silg":
                    return ("g2a" if t < 4 else "g2b", t % 4 // 2), t % 2
                return (("wout", l, t // 2) if l < 2 else ("wout2", t // 2)), t % 2

            def run(j):
                kind, l = j[0], j[1]
                if kind in ("qk", "conv_c", "conv_x", "conv_b", "gate", "silg", "branch", "wout"):
                    ck, m = chunk_of(j)
                    cn, slot = weights(ck)
                    w = ring3(slot, 4 if kind == "branch" else 8)[:, :, m * P:(m + 1) * P]
                    wd = width(l, j[2] if kind == "qk" else "")
                    if kind == "branch":
                        br, d = j[2], j[3]
                        if d == 0 and br == 2:
                            need(oc_ready, ("conv_b", l, 3))
                        elif d == 0:
                            need(oT_ready, ("O", (l, br), len(UNITS[l, br]) // HEADS - 1))
                        product(j, None, w, o4[:, 0 if br == 0 else 1], wd, 4)
                    elif kind == "wout":
                        if j[2] == 0 and l < 2:
                            need(gate_used, ("branch", l, 1, KD - 1))
                        elif j[2] == 0:
                            need(oT_ready, ("O", (2, 0), NX // P - 1))
                            need(oT_ready, ("O", (2, 1), NX // P - 1))
                        product(j, None, w, m3 if l < 2 else o2, wd, KD)
                    else:
                        product(j, (l, "mix"), w, h3, wd, KD)
                    chunk_end[cn] = (job[j][0], job[j][2])
                elif kind == "v":
                    ck, m = chunk_of(j)
                    cn, slot = weights(ck)
                    n, nt = (P, 6) if l < 2 else (P, 4) if j[2] == 0 else (CH, 4)
                    b = begin(j)
                    for t in range(nt):
                        for k in range(KD):
                            mm = pe.matmul(ps[:, b + t * n:b + (t + 1) * n], h3[:, k, t * P:(t + 1) * P],
                                           ring3(slot)[:, k, m * P:m * P + n], start=k == 0, stop=k == KD - 1)
                    part(mm, j)
                    chunk_end[cn] = (job[j][0], job[j][2])
                elif kind == "hs":
                    need(qsq_ready, ("qk",) + j[1:])
                    b = begin(j)
                    for a, e in halves(width(*j[1:])):
                        mm = pe.matmul(ps[:, b + a:b + e], con[:, C_HEAD:C_HEAD + P], sq[:, a:e], start=True, stop=True)
                    part(mm, j)
                elif kind == "rot":
                    need(qn_ready, ("hs",) + j[1:])
                    b = begin(j)
                    part(pe.matmul(ps[:, b:b + NX], con[:, C_ROT:C_ROT + P], qk_dest(*j[1:])[:, 0:NX],
                                   start=True, stop=True), j)
                elif kind == "S":
                    u = UNITS[j[1]][j[2]]
                    q, k, _ = attn_bufs(j[1])
                    if j[2] == 0:
                        need(q_ready, last_rot(j[1]))
                    b = begin(j, j[2] % 2)
                    r = slice(u["half"] * HD, (u["half"] + 1) * HD)
                    for n, (c0, w, k0) in enumerate(u["segs"]):
                        masks = u["masks"] if n == 0 else []
                        mm = pe.matmul(ps[:, b + c0:b + c0 + w], q[r, u["j"], u["q0"]:u["q0"] + P],
                                       k[r, u["kj"], k0:k0 + w], start=True, stop=not masks)
                        for i, (mc, mw, mask) in enumerate(masks):
                            mm = pe.matmul(ps[:, b + mc:b + mc + mw], ident, con[:, C_MASK + mask:C_MASK + mask + mw],
                                           start=False, stop=i == len(masks) - 1)
                    part(mm, j)
                elif kind == "T":
                    need(p_ready, ("S",) + j[1:])
                    b = begin(j, 2)
                    for c0, _ in UNITS[j[1]][j[2]]["tiles"]:
                        mm = pe.transpose(ps[:, b + c0:b + c0 + P], prob[:, j[2] % 2, c0:c0 + P], ident)
                    part(mm, j)
                elif kind == "V":
                    u = UNITS[j[1]][j[2]]
                    v = attn_bufs(j[1])[2]
                    if j[2] == 0:
                        need(v_ready, last_v(j[1]))
                    need(pt_ready[j[2] % 2], ("T",) + j[1:])
                    n = o_number[j[1], j[2] // HEADS]
                    if u["h"] == 0 and n >= 2:
                        pe.wait_ge(o_read.sem, n - 1)
                    b = BANK[3 + n % 2] + u["h"] * HD
                    for i, (c0, t) in enumerate(u["tiles"]):
                        mm = pe.matmul(ps[:, b:b + HD], probT[:, j[2] % 2, c0:c0 + P], v(t, u["vcol"]),
                                       start=i == 0, stop=i == len(u["tiles"]) - 1)
                    mm.then_inc(pv_done.sem, 1)
                elif kind == "O":
                    need(o_read, j)
                    b = begin(j, 2)
                    for n in range(4):
                        mm = pe.transpose(ps[:, b + n * P:b + (n + 1) * P], rs[:, n * P:(n + 1) * P], ident)
                    part(mm, j)

            def experts(l):
                w = NT if l == 0 else NX
                nt = w // P
                key = ("router", l)
                b = begin(key)
                pe.wait_ge(s_router, 16 * (l + 1))
                for t in range(nt):
                    for k in range(KD):
                        if t == 0:
                            need(h_ready, (l, "ffn", k))
                        mm = pe.matmul(ps[:, b + t * E:b + (t + 1) * E], h3[:, k, t * P:(t + 1) * P], wr[:, k, :],
                                       start=k == 0, stop=k == KD - 1)
                part(mm, key)
                for t in range(nt):
                    if t == 2:
                        need(aff_ready, l)
                        b = begin(("affT", l))
                        for s in range(nt):
                            mm = pe.transpose(ps[0:E, b + s * P:b + (s + 1) * P], gates3[:, s, :], ident)
                        part(mm, ("affT", l))
                    b = begin(("tok", l, t))
                    for k in range(KD):
                        mm = pe.transpose(ps[:, b + k * P:b + (k + 1) * P], h3[:, k, t * P:(t + 1) * P], ident)
                    part(mm, ("tok", l, t))
                need(slots_ready, l)
                key = ("route", l)
                b = begin(key)
                for t in range(nt):
                    mm = pe.transpose(ps[:, b + t * E:b + (t + 1) * E], slotm[:, t * P:(t + 1) * P], ident[0:E, 0:E])
                part(mm, key)
                meet()
                open_loop(l)
                C = CX + (CC if l == 0 else 0)

                with pe.Fori(0, PAIRS) as i:
                    def take(key):
                        slot, n, per, _, _ = loop_job[l, key]
                        pe.wait_ge(free[slot], i * per + n)
                        return BANK[slot]

                    def done(mm, key):
                        mm.then_inc(full[loop_job[l, key][0]], 1)

                    def chunk(kind, e, n):
                        slot, value = chunk_at[LOOPC[l] + ROUND.index((kind, e, n))]
                        pe.wait_ge(w_full[slot], i * (16 * len(ROUND) // RING) + value)
                        return ring3(slot)

                    pe.wait_ge(sel_ready, i * SEL[l] + (sel_base[l] + SEL[l]))
                    b = take("gx")
                    for d in range(KD):
                        for t in range(4):
                            mm = pe.matmul(ps[:, b + d * P:b + (d + 1) * P], tok[:, t, d * P:(d + 1) * P],
                                           selx[:, t, :], start=t == 0, stop=t == 3)
                    done(mm, "gx")
                    if l == 0:
                        b = take("gc")
                        for d in range(KD):
                            for t in range(2):
                                mm = pe.matmul(ps[:, b + d * 2 * CC:b + (d + 1) * 2 * CC], tok[:, 4 + t, d * P:(d + 1) * P],
                                               selc[:, t, :], start=t == 0, stop=t == 1)
                        done(mm, "gc")
                    b = take("gt")
                    for t in range(4):
                        mm = pe.transpose(ps[:, b + t * P:b + (t + 1) * P], gselx[:, t, :], ident)
                    if l == 0:
                        for t in range(2):
                            mm = pe.transpose(ps[0:2 * CC, b + 512 + t * P:b + 512 + (t + 1) * P], gselc[:, t, :], ident)
                    done(mm, "gt")
                    pe.wait_ge(xs_ready, i + (1 + PAIRS * l))
                    for e in range(2):
                        for kind in ("eg", "eu"):
                            key = f"{kind}{e}"
                            b = take(key)
                            for n in range(4):
                                wt = chunk(kind, e, n)
                                for f in (2 * n, 2 * n + 1):
                                    o = b + f // 4 * 512 + f % 4 * C
                                    for k in range(KD):
                                        mm = pe.matmul(ps[:, o:o + C], wt[:, k, (f % 2) * P:(f % 2 + 1) * P],
                                                       xs4[:, k, e, 0:C], start=k == 0, stop=k == KD - 1)
                                done(mm, key)
                    for e in range(2):
                        key = f"ed{e}"
                        pe.wait_ge(hm_ready, i * 2 + (1 + e + 2 * PAIRS * l))
                        b = take(key)
                        for n in range(4):
                            wt = chunk("ed", e, n)
                            for k in range(KD):
                                mm = pe.matmul(ps[0:C, b + n * CH:b + (n + 1) * CH], hm2[:, e, k * C:(k + 1) * C], wt[:, k, :],
                                               start=k == 0, stop=k == KD - 1)
                            done(mm, key)
                    pe.wait_ge(gT_ready, i + (1 + PAIRS * l))
                    pe.wait_ge(y_ready, i * 2 + (2 + 2 * PAIRS * l))
                    for d in range(KD):
                        b = take(f"sc{d}")
                        mm = pe.matmul(ps[:, b:b + NX], yx[:, d * P:(d + 1) * P], gTx, start=True, stop=True)
                        if l == 0:
                            mm = pe.matmul(ps[:, b + NX:b + NT], yc[0:2 * CC, d * P:(d + 1) * P], gTc[0:2 * CC, :],
                                           start=True, stop=True)
                        done(mm, f"sc{d}")
                for r in range(PAIRS):
                    for n, (kind, e, p_) in enumerate(ROUND):
                        slot, _, _, f, per = loop_job[l, f"{kind}{e}"]
                        chunk_end[LOOPC[l] + r * len(ROUND) + n] = (slot, f - 3 + p_ + r * per)
                meet()

            pe.wait_ge(s_const, 32)
            pe.wait_ge(s_x, 32)
            for d in range(KD):
                b = begin(("xT", d))
                for t in range(6):
                    mm = pe.transpose(ps[:, b + t * P:b + (t + 1) * P], tok[:, t, d * P:(d + 1) * P], ident)
                part(mm, ("xT", d))
            pe.wait_ge(s_param, PARAM_DMAS * 16)
            for l in range(DEPTH):
                b = begin(("pv", l))
                rows = PROWS[l]
                part(pe.transpose(ps[:, b:b + rows], prob[0:rows, l, 0:P], ident[0:rows, 0:rows]), ("pv", l))
            meet()
            for l in range(DEPTH):
                modulation(l)
                norm_sum((l, "mix"), NT)
                for j in PLAN[l]:
                    run(j)
                meet()
                norm_sum((l, "ffn"), width(l, ""))
                experts(l)
            norm_sum((2, "mix"), NX)
            for j in PLAN[2]:
                run(j)
            meet()
            for t in range(NX // P):
                b = begin(("out", t))
                for k in range(KD):
                    mm = pe.transpose(ps[:, b + k * P:b + (k + 1) * P], xT[:, k, t * P:(t + 1) * P], ident)
                part(mm, ("out", t))

        @block.sync
        def _(sp):
            def load(n):
                slot = n % RING
                if n >= RING:
                    s, value = chunk_end[n - RING]
                    sp.wait_ge(full[s], value)
                for (_, k, cs), src in chunks[n]:
                    sp.dma_start(ring3(slot, k)[:, :, cs], src).then_inc(w_full[slot], 16)

            def round_load(l, i, n, ahead):
                c = LOOPC[l] + n + ahead * len(ROUND)
                kind, e, p_ = ROUND[n]
                s, value = chunk_end[c - RING]
                w = EXPERT_W[kind]
                per_part = [loop_job[l, k][4] for k, _ in loop_plan(l) if loop_job[l, k][0] == s][0]
                sp.wait_ge(full[s], i * per_part + value)
                sp.sem_inc(slot_free, 1)
                at = i * (2 * D * FH) + (((l * E + 2 * ahead + e) * D) * FH + p_ * CH)
                src = bass.AP(w.tensor, at, [[FH, P], [P * FH, KD], [1, CH]])
                sp.dma_start(ring3(c % RING), src).then_inc(w_full[c % RING], 16)

            end = 0
            for l in range(DEPTH):
                for n in range(end, LOOPC[l] + RING):
                    load(n)
                with sp.Fori(0, PAIRS - 1) as i:
                    for n in range(RING, len(ROUND)):
                        round_load(l, i, n, 0)
                    for n in range(RING):
                        round_load(l, i, n, 1)
                end = LOOPC[l] + PAIRS * len(ROUND)
                for n in range(end - len(ROUND) + RING, end):
                    load(n)
            for n in range(end, len(chunks)):
                load(n)

        @block.gpsimd
        def _(pool):
            phases = [0]

            def meet():
                phases[0] += 1
                pool.sem_inc(s_phase, 1)
                pool.wait_ge(s_phase, 4 * phases[0])

            pool.dma_start(con[:, 0:C_COS], consts[:, 0:C_COS]).then_inc(s_const, 16)
            pool.dma_start(con[:, C_COS:C_COS2], consts[:, C_COS:C_COS2]).then_inc(s_const, 16)
            pool.dma_start(tok[:, 0:4, :], x[0].rearrange("(t p) d -> p t d", p=P)).then_inc(s_x, 16)
            pool.dma_start(tok[:, 4:6, :], ctx_in[0].rearrange("(t p) d -> p t d", p=P)).then_inc(s_x, 16)
            n_param = [0]

            def param(dst, src):
                n_param[0] += 1
                pool.dma_start(dst, src).then_inc(s_param, 16)

            def rows(l, r0, vec):
                n = vec.shape[0] // P
                param(prob[r0:r0 + n, l, 0:P], vec.rearrange("(k p) -> k p", p=P))

            for l in range(DEPTH):
                rows(l, PB_ADA, b_ada[l])
                rows(l, PG_MIX, g_mix[l])
                rows(l, PG_FFN, g_ffn[l])
                param(prob[PCONV:PCONV + 12, l, 0:P], conv_w[l].rearrange("j (k p) -> (j k) p", p=P))
                for n, g in enumerate((qg_a, kg_a, qg_b, kg_b)):
                    for r in range(2):
                        param(prob[PQK + n:PQK + n + 1, l, r * HD:(r + 1) * HD], g[l:l + 1, :])
                param(sinks[:, l, :], sink_b[l].partition_broadcast(P))
            rows(0, PEXTRA, c[0])
            rows(0, PEXTRA + 8, c_ctx)
            rows(1, PEXTRA, norm_gain_2[0])
            for n, g in enumerate((q_norm_a_2, k_norm_a_2, q_norm_b_2, k_norm_b_2)):
                for r in range(2):
                    param(prob[PEXTRA + 8 + n:PEXTRA + 9 + n, 1, r * HD:(r + 1) * HD], g)
            param(sinks[:, 2, :], sinks_a_2[0].partition_broadcast(P))
            assert n_param[0] == PARAM_DMAS, n_param
            pool.dma_start(wr[:, :, :], w_router[0].rearrange("(k p) e -> p k e", p=P)).then_inc(s_router, 16)
            meet()
            for l in range(DEPTH):
                meet()
                meet()
                meet()
                if l == 0:
                    pool.dma_start(wr[:, :, :], w_router[1].rearrange("(k p) e -> p k e", p=P)).then_inc(s_router, 16)
                else:
                    pool.dma_start(con[:, C_COS:C_COS2], consts[:, C_COS2:C_END]).then_inc(s_rope2, 16)
            meet()
            for t in range(NX // P):
                pool.wait_ge(out_copied.sem, out_copied.at[t])
                pool.dma_start(out[0, t * P:(t + 1) * P, :], tok[:, t, :]).then_inc(s_out, 16)
            pool.wait_ge(s_out, 16 * (NX // P))

        class Engine:

            def __init__(self, eng, step_sem):
                self.eng, self.step, self.n, self.phases = eng, step_sem, 0, 0

            def do(self, ins, ev=None, key=None):
                if ev is None:
                    self.n += 1
                    ins.then_inc(self.step, 1)
                    self.eng.wait_ge(self.step, self.n)
                else:
                    ins.then_inc(ev.sem, 1)
                    self.eng.wait_ge(ev.sem, ev.at[key])

            def need(self, ev, key):
                self.eng.wait_ge(ev.sem, ev.at[key])

            def read(self, key):
                slot, _, value = job[key]
                self.eng.wait_ge(full[slot], value)
                return BANK[slot]

            def release(self, key):
                self.eng.sem_inc(free[job[key][0]], 1)

            def meet(self):
                self.phases += 1
                self.eng.sem_inc(s_phase, 1)
                self.eng.wait_ge(s_phase, 4 * self.phases)

        @block.scalar
        def _(act):
            A = Engine(act, act_step)
            sc = nc.scalar

            def func(o, i, f, **kw):
                return sc.activation(o, i, f, **kw)

            for d in range(0, KD, 2):
                b = A.read(("xT", d))
                A.do(sc.copy(xT[:, d, :], ps[:, b:b + NT]))
                A.release(("xT", d))
            act.wait_ge(pv_ready, 1)
            func(tmpc[:, :], pv[:, 0, PEXTRA:PEXTRA + 2 * KD], ACT.Sigmoid).then_inc(sil_sig, 1)
            act.wait_ge(sil_sig, 1)
            A.meet()

            last_rs = [None]

            def root(key, w, n):
                b = A.read(key)
                A.do(func(rs[:, 0:w], ps[:, b:b + w], ACT.Sqrt, bias=epsn[:, n == D:(n == D) + 1]), rms_ready, key)
                A.release(key)

            def norm(ph, w):
                l = ph[0]
                for d in range(KD):
                    A.do(func(m3[:, d, 0:w], xT[:, d, 0:w], ACT.Square), sq_ready, ("n",) + ph + (d,))
                root(("norm",) + ph, w, D)
                last_rs[0] = (hpre, ph + (KD - 1,))
                sh = (SH1 if ph[1] == "mix" else SH2)
                for d in range(KD):
                    A.need(hpre, ph + (d,))
                    for a, e in halves(w):
                        shift = zero3[:, d, 0:1] if l == 2 else mod3[:, sh + d, a // 512:a // 512 + 1]
                        ins = func(h3[:, d, a:e], h3[:, d, a:e], ACT.Identity, bias=shift)
                        if e == w:
                            A.do(ins, h_ready, ph + (d,))
                        else:
                            A.do(ins)

            last_hs = [None]

            def run(j):
                kind, l = j[0], j[1]
                if kind == "qk":
                    w = width(l, j[2])
                    b = A.read(j)
                    if last_hs[0]:
                        A.read(last_hs[0])
                    A.do(func(sq[:, 0:w], ps[:, b:b + w], ACT.Square), qsq_ready, j)
                    last_hs[0] = ("hs",) + j[1:]
                elif kind == "hs":
                    A.need(*last_rs[0])
                    root(j, width(*j[1:]), HD)
                elif kind == "rot":
                    last_rs[0] = (q_ready, j)
                elif kind == "v":
                    b = A.read(j)
                    if l < 2:
                        A.do(sc.copy(v4[:, j[2]], ps[:, b:b + NT].rearrange("p (t f) -> p t f", f=P)), v_ready, j)
                    else:
                        n, f0 = (P, 0) if j[2] == 0 else (CH, P + CH * (j[2] - 1))
                        A.do(sc.copy(v2[:, :, f0:f0 + n], ps[:, b:b + 4 * n].rearrange("p (t f) -> p t f", f=n)), v_ready, j)
                    A.release(j)
                elif kind == "conv_c":
                    w = width(l, "")
                    b = A.read(j)
                    if j[2] >= 2:
                        A.need(cu_used, ("conv_x", l, j[2] - 2))
                    A.do(sc.copy(prob[:, j[2] % 2, 0:w], ps[:, b:b + w]), cg_ready, j)
                    A.release(j)
                elif kind in ("gate", "silg"):
                    w = width(l, "")
                    n = j[3] if kind == "gate" else j[2]
                    b = A.read(j)
                    if kind == "gate" and n == 0 and j[2] in (2, 0):
                        A.need(pv_done, ("V", (l, 0 if j[2] == 2 else 1), len(UNITS[l, 0 if j[2] == 2 else 1]) - 1))
                    if kind == "gate" and n >= 2:
                        A.need(gate_used, ("branch", l, j[2], n - 2))
                    elif kind == "gate" and j[2] == 1:
                        A.need(gate_used, ("branch", l, 0, KD - 2 + n))
                    elif kind == "silg" and n >= 2:
                        A.need(gate_used, ("silg", l, n - 2))
                    A.do(func(probT[:, n % 2, 0:w], ps[:, b:b + w], ACT.Sigmoid), sig_ready, j)
                    if kind == "gate":
                        A.release(j)
                elif kind == "S":
                    u = UNITS[j[1]][j[2]]
                    lo, hi, h = u["lo"], u["hi"], u["h"]
                    b = A.read(j)
                    A.need(nm_ready, j)
                    if j[2] >= 2:
                        A.read(("T", j[1], j[2] - 2))
                    A.do(func(prob[:, j[2] % 2, lo:hi], ps[:, b + lo:b + hi], ACT.Exp, bias=nms[:, u["qt"] % 2, h:h + 1],
                              scale=SCALE, accum_out=lsum[:, u["qt"] % 2, h:h + 1]), p_ready, j)
                    A.release(j)
                    if h == HEADS - 1 and j[1] in SINK:
                        o = ("O", j[1], u["qt"])
                        A.need(sd_ready, o)
                        A.do(func(sexp[:, :], sdif[:, :], ACT.Exp), se_ready, o)
                elif kind == "T" and j[2] % 2 == 0:
                    u = UNITS[j[1]][j[2]]
                    b = A.read(j)
                    if j[2] == 0 and j[1][1] == 1 and j[1][0] < 2:
                        A.need(gate_used, ("branch", j[1][0], 2, KD - 1))
                    elif j[2] == 0 and j[1] == (2, 0):
                        A.need(gate_used, ("silg", 2, KD - 1))
                    if j[2] >= 2:
                        A.need(pv_done, ("V", j[1], j[2] - 2))
                    A.do(sc.copy(probT[:, 0, u["lo"]:u["hi"]], ps[:, b + u["lo"]:b + u["hi"]]), pt_ready[0], j)
                    A.release(j)
                elif kind == "O" and j[1][0] < 2:
                    l, br = j[1]
                    b = A.read(j)
                    if br == 1 and j[2] == 0:
                        A.read(("branch", l, 2, KD - 1))
                    A.do(sc.copy(o4[:, br, :, j[2] * P:(j[2] + 1) * P], ps[:, b:b + 512].rearrange("p (k t) -> p k t", k=4)),
                         oT_ready, j)
                    A.release(j)

            def experts(l):
                w = width(l, "")
                A.need(aff_max, l)
                A.do(func(gates3[:, 0:w // P, :], gates3[:, 0:w // P, :], ACT.Exp), aff_exp, l)
                for t in range(w // P):
                    b = A.read(("tok", l, t))
                    A.do(sc.copy(tok[:, t, :], ps[:, b:b + D]))
                    A.release(("tok", l, t))
                A.meet()
                C = CX + (CC if l == 0 else 0)
                per_round = (1 if l == 0 else 0) + (1 if l == 0 else 0) + (2 if l == 0 else 0)
                with act.Fori(0, PAIRS) as i:
                    count = [0]

                    def step(ins):
                        count[0] += 1
                        ins.then_inc(act_step, 1)
                        act.wait_ge(act_step, i * per_round + (A.n + count[0]))

                    def read(key):
                        slot, _, _, f, per = loop_job[l, key]
                        act.wait_ge(full[slot], i * per + f)
                        return BANK[slot]

                    def release(key):
                        act.sem_inc(free[loop_job[l, key][0]], 1)

                    b = read("gx")
                    if l == 0:
                        b2 = read("gc")
                        step(sc.copy(xs4[:, :, :, CX:C], ps[:, b2:b2 + 512].rearrange("p (k e c) -> p k e c", k=KD, e=2)))
                        release("gc")
                    sc.copy(xs4[:, :, :, 0:CX], ps[:, b:b + D].rearrange("p (k e c) -> p k e c", k=KD, e=2)).then_inc(xs_ready, 1)
                    act.wait_ge(xs_ready, i + (1 + PAIRS * l))
                    release("gx")
                    b = read("gt")
                    if l == 0:
                        step(sc.copy(gTc[0:2 * CC, :], ps[0:2 * CC, b + 512:b + NT]))
                    sc.copy(gTx, ps[:, b:b + NX]).then_inc(gT_ready, 1)
                    act.wait_ge(gT_ready, i + (1 + PAIRS * l))
                    release("gt")
                    for e in range(2):
                        b = read(f"eg{e}")
                        v = ps[:, b:b + 1024].rearrange("p (g f) -> p g f", g=2)[:, :, 0:4 * C]
                        func(eg2[:, e, 0:8 * C].rearrange("p (g f) -> p g f", g=2), v, ACT.Sigmoid).then_inc(eg_sig, 1)
                        act.wait_ge(eg_sig, i * 2 + (1 + e + 2 * PAIRS * l))
                    for e in range(2):
                        b = read(f"ed{e}")
                        if l == 0:
                            step(sc.copy(yc[CC * e:CC * (e + 1), :], ps[CX:C, b:b + D]))
                        sc.copy(yx[CX * e:CX * (e + 1), :], ps[0:CX, b:b + D]).then_inc(y_ready, 1)
                        act.wait_ge(y_ready, i * 2 + (1 + e + 2 * PAIRS * l))
                        release(f"ed{e}")
                    assert count[0] == per_round
                A.n += PAIRS * per_round
                A.meet()

            for l in range(DEPTH):
                A.need(ada_done, l)
                norm((l, "mix"), NT)
                for j in PLAN[l]:
                    run(j)
                A.meet()
                norm((l, "ffn"), width(l, ""))
                experts(l)
            norm((2, "mix"), NX)
            for j in PLAN[2]:
                run(j)
            A.meet()
            for t in range(NX // P):
                b = A.read(("out", t))
                A.do(sc.copy(tok[:, t, :], ps[:, b:b + D]), out_copied, t)
                A.release(("out", t))

        @block.vector
        def _(dve):
            V = Engine(dve, dve_step)
            v = nc.vector

            V.do(v.memset(ones[:, :], 1.0))
            V.do(v.memset(route[:, :], 0.0))
            V.do(v.memset(epsn[:, 0:1], HD * EPS))
            V.do(v.memset(epsn[:, 1:2], D * EPS))
            V.do(v.memset(zero2[:, :], 0.0))
            for d in range(1, KD, 2):
                b = V.read(("xT", d))
                V.do(v.tensor_copy(xT[:, d, :], ps[:, b:b + NT]))
                V.release(("xT", d))
            for l in range(DEPTH):
                b = V.read(("pv", l))
                if l == 0:
                    v.tensor_copy(pv[:, l, 0:PROWS[l]], ps[:, b:b + PROWS[l]]).then_inc(pv_ready, 1)
                    dve.wait_ge(pv_ready, 1)
                else:
                    V.do(v.tensor_copy(pv[:, l, 0:PROWS[l]], ps[:, b:b + PROWS[l]]))
                V.release(("pv", l))
                V.do(v.tensor_scalar(pv[:, l, PQK:PQK + 4], pv[:, l, PQK:PQK + 4], HD ** 0.5, None, ALU.mult))
            V.do(v.tensor_scalar(pv[:, 1, PEXTRA + 8:PEXTRA + 12], pv[:, 1, PEXTRA + 8:PEXTRA + 12], HD ** 0.5, None, ALU.mult))
            V.do(v.tensor_scalar(nsink[:, :, :], sinks[:, :, :], -1.0, None, ALU.mult))
            dve.wait_ge(sil_sig, 1)
            v.tensor_tensor(silc[:, :], tmpc[:, :], pv[:, 0, PEXTRA:PEXTRA + 2 * KD], ALU.mult).then_inc(sil_ready, 1)
            dve.wait_ge(sil_ready, 1)
            V.meet()

            def modulation(l):
                key = ("ada", l)
                b = V.read(key)
                V.do(v.tensor_tensor(mod3[:, :, :], ps[:, b:b + 96].rearrange("p (k w) -> p k w", w=2),
                                     pv[:, l, PB_ADA:PB_ADA + 48].unsqueeze(2).broadcast_to([P, 48, 2]), ALU.add))
                V.release(key)
                for n, (sc_, g) in enumerate(((SC1, PG_MIX), (SC2, PG_FFN))):
                    gain = pv[:, l, g:g + KD].unsqueeze(2).broadcast_to([P, KD, 2])
                    V.do(v.scalar_tensor_tensor(amp4[:, n], mod3[:, sc_:sc_ + KD, :], 1.0, gain, ALU.add, ALU.mult))
                    ins = v.tensor_scalar(amp4[:, n], amp4[:, n], D ** 0.5, None, ALU.mult)
                    if n == 0:
                        V.do(ins)
                    else:
                        V.do(ins, ada_done, l)

            def norm(ph, w):
                key = ("norm",) + ph
                V.need(rms_ready, key)
                V.do(v.reciprocal(rs[:, 0:w], rs[:, 0:w]))
                for d in range(KD):
                    for a, e in halves(w):
                        ins = v.scalar_tensor_tensor(h3[:, d, a:e], xT[:, d, a:e],
                                                     amp4[:, ph[1] == "ffn", d, a // 512:a // 512 + 1],
                                                     rs[:, a:e], ALU.mult, ALU.mult)
                        if e == w:
                            V.do(ins, hpre, ph + (d,))
                        else:
                            V.do(ins)

            def run(j):
                kind, l = j[0], j[1]
                w = width(l, j[2] if kind in ("qk", "hs") else "") if kind not in ("S", "T", "V", "O") else 0
                if kind == "qk":
                    b = V.read(j)
                    V.need(qsq_ready, j)
                    V.do(v.tensor_copy(qk_dest(*j[1:])[:, 0:w], ps[:, b:b + w]))
                    V.release(j)
                elif kind == "hs":
                    V.need(rms_ready, j)
                    V.do(v.reciprocal(rs[:, 0:w], rs[:, 0:w]))
                    t = qk_dest(*j[1:])[:, 0:w]
                    V.do(v.scalar_tensor_tensor(t, t, gain_col(*j[1:]), rs[:, 0:w], ALU.mult, ALU.mult), qn_ready, j)
                elif kind == "rot":
                    t = qk_dest(*j[1:])[:, 0:NX]
                    b = V.read(j)
                    V.do(v.tensor_tensor(rs[:, 0:NX], ps[:, b:b + NX], con[:, C_SIN:C_SIN + NX], ALU.mult))
                    V.release(j)
                    V.do(v.tensor_tensor(t, t, con[:, C_COS:C_COS + NX], ALU.mult))
                    V.do(v.tensor_tensor(t, t, rs[:, 0:NX], ALU.add), q_ready, j)
                elif kind == "conv_x":
                    m = j[2]
                    u, y = prob[:, m % 2], o4[:, 1, m]
                    tap = [pv[:, l, PCONV + 4 * t + m:PCONV + 4 * t + m + 1] for t in range(3)]
                    V.need(cg_ready, ("conv_c", l, m))
                    b = V.read(j)
                    V.do(v.tensor_tensor(u[:, 0:w], u[:, 0:w], ps[:, b:b + w], ALU.mult))
                    V.release(j)
                    V.do(v.tensor_scalar(y[:, 0:w], u[:, 0:w], tap[1], None, ALU.mult))
                    for a, e in halves(w):
                        V.do(v.scalar_tensor_tensor(y[:, a + 1:e], u[:, a:e - 1], tap[0], y[:, a + 1:e], ALU.mult, ALU.add))
                        ins = v.scalar_tensor_tensor(y[:, a:e - 1], u[:, a + 1:e], tap[2], y[:, a:e - 1], ALU.mult, ALU.add)
                        if e == w:
                            V.do(ins, cu_used, j)
                        else:
                            V.do(ins)
                elif kind == "conv_b":
                    y = o4[:, 1, j[2]]
                    b = V.read(j)
                    V.do(v.tensor_tensor(y[:, 0:w], y[:, 0:w], ps[:, b:b + w], ALU.mult), oc_ready, j)
                    V.release(j)
                elif kind == "branch":
                    br, d = j[2], j[3]
                    g = probT[:, d % 2, 0:w]
                    V.need(sig_ready, ("gate", l, br, d))
                    b = V.read(j)
                    if br == 2:
                        V.do(v.tensor_tensor(m3[:, d, 0:w], g, ps[:, b:b + w], ALU.mult), gate_used, j)
                        V.release(j)
                    else:
                        V.do(v.tensor_tensor(g, g, ps[:, b:b + w], ALU.mult))
                        V.release(j)
                        V.do(v.tensor_tensor(m3[:, d, 0:w], m3[:, d, 0:w], g, ALU.add), gate_used, j)
                elif kind == "silg":
                    d = j[2]
                    g = probT[:, d % 2, 0:w]
                    V.need(sig_ready, j)
                    b = V.read(j)
                    V.do(v.tensor_tensor(sg2[:, d, :], g, ps[:, b:b + w], ALU.mult), gate_used, j)
                    V.release(j)
                elif kind == "wout":
                    d = j[2]
                    b = V.read(j)
                    for a, e in halves(w):
                        if l < 2:
                            V.do(v.scalar_tensor_tensor(xT[:, d, a:e], ps[:, b + a:b + e],
                                                        mod3[:, GT1 + d, a // 512:a // 512 + 1], xT[:, d, a:e],
                                                        ALU.mult, ALU.add))
                        else:
                            V.do(v.tensor_tensor(xT[:, d, a:e], xT[:, d, a:e], ps[:, b + a:b + e], ALU.add))
                    V.release(j)
                elif kind == "S":
                    u = UNITS[j[1]][j[2]]
                    h, p2 = u["h"], u["qt"] % 2
                    b = V.read(j)
                    V.do(v.tensor_reduce(mxn[:, h:h + 1], ps[:, b + u["lo"]:b + u["hi"]], AX.X, ALU.max, negate=True))
                    if j[1] in SINK:
                        V.do(v.tensor_scalar(nms[:, p2, h:h + 1], mxn[:, h:h + 1], SCALE, nsink[:, SINK[j[1]], h:h + 1],
                                             ALU.mult, ALU.min), nm_ready, j)
                        if h == HEADS - 1:
                            o = ("O", j[1], u["qt"])
                            if o_number[o[1:]] and se_before(o):
                                V.need(se_ready, se_before(o))
                            V.do(v.tensor_tensor(sdif[:, :], sinks[:, SINK[j[1]], :], nms[:, p2, :], ALU.add), sd_ready, o)
                    else:
                        V.do(v.tensor_scalar(nms[:, p2, h:h + 1], mxn[:, h:h + 1], SCALE, None, ALU.mult), nm_ready, j)
                elif kind == "T" and j[2] % 2 == 1:
                    u = UNITS[j[1]][j[2]]
                    b = V.read(j)
                    if j[2] >= 2:
                        V.need(pv_done, ("V", j[1], j[2] - 2))
                    V.do(v.tensor_copy(probT[:, 1, u["lo"]:u["hi"]], ps[:, b + u["lo"]:b + u["hi"]]), pt_ready[1], j)
                    V.release(j)
                elif kind == "V" and UNITS[j[1]][j[2]]["h"] == HEADS - 1:
                    qt = j[2] // HEADS
                    p2, o = qt % 2, ("O", j[1], j[2] // HEADS)
                    V.need(p_ready, ("S",) + j[1:])
                    den = lsum[:, p2, :]
                    if j[1] in SINK:
                        V.need(se_ready, o)
                        V.do(v.tensor_tensor(den, den, sexp[:, :], ALU.add))
                    V.do(v.reciprocal(den, den))
                    V.need(pv_done, j)
                    b = BANK[3 + o_number[o[1:]] % 2]
                    V.do(v.tensor_tensor(rs[:, 0:512].rearrange("p (h f) -> p h f", h=HEADS),
                                         ps[:, b:b + 512].rearrange("p (h f) -> p h f", h=HEADS),
                                         den.unsqueeze(2).broadcast_to([P, HEADS, HD]), ALU.mult), o_read, o)
                elif kind == "O":
                    b = V.read(j)
                    if j[1][0] == 2:
                        t0 = 4 * j[1][1]
                        tt = slice(j[2] * P, (j[2] + 1) * P)
                        V.do(v.tensor_tensor(o2[:, t0:t0 + 4, tt], sg2[:, t0:t0 + 4, tt],
                                             ps[:, b:b + 512].rearrange("p (k t) -> p k t", k=4), ALU.mult), oT_ready, j)
                        V.release(j)

            def se_before(o):
                n = with_sink.index(o)
                return with_sink[n - 1] if n else None

            def experts(l):
                w = width(l, "")
                segs = halves(w)
                nt = w // P
                b = V.read(("router", l))
                logits = ps[:, b:b + nt * E].rearrange("p (t e) -> p t e", t=nt)
                gates = gates3[:, 0:nt, :]

                def of_token(stat):
                    return stat[:, 0:nt].unsqueeze(2).broadcast_to([P, nt, E])

                V.do(v.tensor_reduce(mxn[:, 0:nt], logits, AX.X, ALU.max))
                V.do(v.tensor_tensor(gates, logits, of_token(mxn), ALU.subtract), aff_max, l)
                V.release(("router", l))
                V.do(v.memset(rone[:, 0:w], 1.0))
                V.need(aff_exp, l)
                V.do(v.tensor_reduce(sdif[:, 0:nt], gates, AX.X, ALU.add))
                V.do(v.reciprocal(sdif[:, 0:nt], sdif[:, 0:nt]))
                V.do(v.tensor_tensor(gates, gates, of_token(sdif), ALU.mult), aff_ready, l)
                b = V.read(("affT", l))
                V.do(v.tensor_copy(work[:, 0:w], ps[0:E, b:b + w]))
                V.release(("affT", l))
                for n, (a, e) in enumerate(segs):
                    for _ in range((CX, CC)[n] // 8):
                        V.do(v.max(m8[:, :], work[:, a:e]))
                        V.do(v.match_replace(work[:, a:e], m8[:, :], work[:, a:e], -1.0))
                V.do(v.tensor_scalar(selm[:, 0:w], work[:, 0:w], 0.0, None, ALU.is_lt))
                for a, e in segs:
                    V.do(v.tensor_tensor_scan(slotm[:, a:e], rone[:, a:e], selm[:, a:e], 0.0, ALU.mult, ALU.add))
                V.do(v.tensor_tensor(slotm[:, 0:w], slotm[:, 0:w], selm[:, 0:w], ALU.mult))
                V.do(v.tensor_scalar(slotm[:, 0:w], slotm[:, 0:w], -1.0, None, ALU.add), slots_ready, l)
                key = ("route", l)
                b = V.read(key)
                V.do(v.tensor_copy(route[:, 0:nt * E], ps[:, b:b + nt * E]))
                V.release(key)
                V.meet()
                C = CX + (CC if l == 0 else 0)
                per_round = 2 + KD * len(segs)
                
                def pair_of(n, t0, tiles, e0):
                    lo = (6 * n + t0) * E
                    return bass.AP(route[:, :].tensor, e0 + lo, [[12 * E + 2, P], [E, tiles], [1, 2]])

                def select(e0, before):
                    n = 0
                    for tiles, t0, cap, sel, gsel in ((4, 0, CX, selx, gselx), (2, 4, CC, selc, gselc))[:2 - l]:
                        shape = [P, tiles, 2, cap]
                        s4 = sel.rearrange("p t (e c) -> p t e c", e=2)
                        g4 = gsel.rearrange("p t (e c) -> p t e c", e=2)
                        slot, gate = (pair_of(n_, t0, tiles, e0).unsqueeze(3).broadcast_to(shape) for n_ in range(2))
                        iota = con[:, C_IOTA:C_IOTA + cap].unsqueeze(1).unsqueeze(1).broadcast_to(shape)
                        v.tensor_tensor(s4, iota, slot, ALU.is_equal).then_inc(sel_ready, 1)
                        dve.wait_ge(sel_ready, before + (n + 1))
                        v.tensor_tensor(g4, s4, gate, ALU.mult).then_inc(sel_ready, 1)
                        dve.wait_ge(sel_ready, before + (n + 2))
                        n += 2

                select(0, sel_base[l])
                with dve.Fori(0, PAIRS) as i:
                    count = [0]

                    def step(ins):
                        count[0] += 1
                        ins.then_inc(dve_step, 1)
                        dve.wait_ge(dve_step, i * per_round + (V.n + count[0]))

                    def read(key):
                        slot, _, _, f, per = loop_job[l, key]
                        dve.wait_ge(full[slot], i * per + f)
                        return BANK[slot]

                    def release(key):
                        dve.sem_inc(free[loop_job[l, key][0]], 1)

                    def hidden(key):
                        b = read(key)
                        return ps[:, b:b + 1024].rearrange("p (g f) -> p g f", g=2)[:, :, 0:4 * C]

                    for e in range(2):
                        g = eg2[:, e, 0:8 * C].rearrange("p (g f) -> p g f", g=2)
                        hm = hm2[:, e, 0:8 * C].rearrange("p (g f) -> p g f", g=2)
                        dve.wait_ge(eg_sig, i * 2 + (1 + e + 2 * PAIRS * l))
                        step(v.tensor_tensor(g, g, hidden(f"eg{e}"), ALU.mult))
                        release(f"eg{e}")
                        v.tensor_tensor(hm, g, hidden(f"eu{e}"), ALU.mult).then_inc(hm_ready, 1)
                        dve.wait_ge(hm_ready, i * 2 + (1 + e + 2 * PAIRS * l))
                        release(f"eu{e}")
                    read("gt")
                    select(i * 2 + 2, i * SEL[l] + (sel_base[l] + SEL[l]))
                    for d in range(KD):
                        b = read(f"sc{d}")
                        for a, e in segs:
                            step(v.scalar_tensor_tensor(xT[:, d, a:e], ps[:, b + a:b + e],
                                                        mod3[:, GT2 + d, a // 512:a // 512 + 1], xT[:, d, a:e],
                                                        ALU.mult, ALU.add))
                        release(f"sc{d}")
                    assert count[0] == per_round, count
                V.n += PAIRS * per_round
                V.meet()

            for l in range(DEPTH):
                modulation(l)
                norm((l, "mix"), NT)
                for j in PLAN[l]:
                    run(j)
                V.meet()
                norm((l, "ffn"), width(l, ""))
                experts(l)
            V.do(v.tensor_scalar(amp4[:, 0, :, 0], pv[:, 1, PEXTRA:PEXTRA + KD], D ** 0.5, None, ALU.mult))
            dve.wait_ge(s_rope2, 16)
            norm((2, "mix"), NX)
            for j in PLAN[2]:
                run(j)
            V.meet()


_INS = ["x", "c", "ctx", "c_ctx", "w_ada", "b_ada", "g_mix", "g_ffn", "w_in", "qg_a", "kg_a", "qg_b", "kg_b", "sink_b",
        "conv_w", "w_branch", "w_out", "w_router", "w_e_gate", "w_e_up", "w_e_down", "norm_gain_2", "w_in_2",
        "q_norm_a_2", "k_norm_a_2", "sinks_a_2", "q_norm_b_2", "k_norm_b_2", "w_out_2"]


def kernel(**inputs):
    import concourse.bacc as bacc
    from concourse.bass_utils import run_bass_kernel_spmd

    nc = bacc.Bacc("TRN2", target_bir_lowering=False, num_devices=1)
    arrays, args = {}, []
    for name in _INS + ["consts"]:
        a = constants() if name == "consts" else np.ascontiguousarray(inputs[name])
        arrays[f"in_{name}"] = a
        args.append(nc.dram_tensor(f"in_{name}", a.shape, mybir.dt.from_np(a.dtype), kind="ExternalInput").ap())
    args.append(nc.dram_tensor("out_x", (1, NX, D), F32, kind="ExternalOutput").ap())
    program(nc, *args)
    return run_bass_kernel_spmd(nc, [arrays], core_ids=[0]).results[0]["out_x"]
```

```python
from contextlib import ExitStack

import numpy as np

import concourse.bass as bass
from concourse import mybir

F32 = mybir.dt.float32
ALU = mybir.AluOpType
ACT = mybir.ActivationFunctionType
AX = mybir.AxisListType

P = 128
D = 1024
KD = D // P
NX, NC = 512, 256
NT = NX + NC
DEPTH = 2
HD = 64
HEADS = 8
EPS = 1e-6
E = 16
FH = 1024
QUAD = 4
CX, CC = 2 * NX // E, 2 * NC // E
SCALE = HD ** -0.5
NEG = -1e30

CH = 256
RING = 6

KV_END, OFF_QA, OFF_QB, OFF_CONV, OFF_GATE = 512, 512, 1024, 1536, 3072
Q2A, K2A, G2A, Q2B, K2B, V2B, G2B, W2 = 0, 512, 768, 1280, 1792, 2304, 2816, 3328

PB_ADA, PG_MIX, PG_FFN, PCONV, PQK, PEXTRA = 0, 48, 56, 64, 76, 80
SH1, SC1, GT1, SH2, SC2, GT2 = (8 * j for j in range(6))

C_ID, C_ROT, C_HEAD, C_MASK, C_IOTA, C_COS, C_SIN, C_COS2, C_SIN2, C_END = (
    0, 128, 256, 384, 384 + 8 * P, 384 + 8 * P + CX, 384 + 8 * P + CX + NX,
    384 + 8 * P + CX + 2 * NX, 384 + 8 * P + CX + 3 * NX, 384 + 8 * P + CX + 4 * NX)
PROWS = (96, 92)
M_DIL, M_BAND, M_PREV, M_NEXT = 0, 4 * P, 6 * P, 7 * P


def constants():
    c = np.zeros((P, C_END), np.float32)
    c[:, C_ID:C_ID + P] = np.eye(P)
    for f in range(P):
        h, r = f // HD * HD, f % HD
        if r < HD // 2:
            c[h + r + HD // 2, C_ROT + f] = -1.0
        else:
            c[h + r - HD // 2, C_ROT + f] = 1.0
        c[h:h + HD, C_HEAD + f] = 1.0
    q, k = np.arange(P)[:, None], np.arange(P)[None, :]
    for n, b in enumerate((2, 2, 1, 0)):
        dist = P * b + q - k
        count = ((dist >= 0) & (dist <= 128)) * 1 + ((dist >= 0) & (dist % 4 == 0)) + ((dist >= 0) & (dist % 16 == 0))
        c[:, C_MASK + M_DIL + n * P:C_MASK + M_DIL + (n + 1) * P] = np.where(
            count > 0, np.log(np.maximum(count, 1)) / SCALE, NEG)
    c[:, C_MASK + M_BAND:C_MASK + M_BAND + P] = np.where(k > q, 0, NEG)
    c[:, C_MASK + M_BAND + P:C_MASK + M_BAND + 2 * P] = np.where(k <= q, 0, NEG)
    c[:, C_MASK + M_PREV:C_MASK + M_PREV + P] = np.where(k >= q, 0, NEG)
    c[:, C_MASK + M_NEXT:C_MASK + M_NEXT + P] = np.where(k <= q, 0, NEG)
    c[:, C_IOTA:C_IOTA + CX] = np.arange(CX)
    n4 = HD // 4
    inv = np.float32(10000.0) ** (-np.arange(n4, dtype=np.float32) / np.float32(n4))
    t = np.arange(NX)
    ang = np.concatenate([(t // 64).astype(np.float32)[:, None] * inv, (t % 64).astype(np.float32)[:, None] * inv], 1)
    n2 = HD // 2
    inv2 = np.float32(10000.0) ** (-np.arange(n2, dtype=np.float32) / np.float32(n2))
    ang2 = t.astype(np.float32)[:, None] * inv2
    for f in range(P):
        c[f, C_COS:C_COS + NX] = np.cos(ang[:, f % n2])
        c[f, C_SIN:C_SIN + NX] = np.sin(ang[:, f % n2])
        c[f, C_COS2:C_COS2 + NX] = np.cos(ang2[:, f % n2])
        c[f, C_SIN2:C_SIN2 + NX] = np.sin(ang2[:, f % n2])
    return c


class Count:

    def __init__(self, sem, keys):
        self.sem, self.at = sem, {k: n + 1 for n, k in enumerate(keys)}
        assert len(self.at) == len(keys)


def program(nc, x, c, ctx_in, c_ctx, w_ada, b_ada, g_mix, g_ffn, w_in, qg_a, kg_a, qg_b, kg_b, sink_b, conv_w,
            w_branch, w_out, w_router, w_e_gate, w_e_up, w_e_down, norm_gain_2, w_in_2, q_norm_a_2, k_norm_a_2,
            sinks_a_2, q_norm_b_2, k_norm_b_2, w_out_2, consts, out):
    with ExitStack() as stack:
        def sb(name, shape):
            return stack.enter_context(nc.sbuf_tensor(name, shape, F32))

        def sem(name):
            return stack.enter_context(nc.semaphore(name))

        ps = stack.enter_context(nc.psum_tensor("ps", [P, 8 * 512], F32))
        ring = sb("ring", [P, RING, 8 * CH])
        xT = sb("xT", [P, KD, NT])
        hT = sb("hT", [P, KD * NT])
        merged = sb("merged", [P, KD * NT])
        qbuf = sb("qbuf", [P, 4 * NT])
        obuf = sb("obuf", [P, 8 * NT])
        kbuf = sb("kbuf", [P, 2 * NT])
        vbuf = sb("vbuf", [P, 2560])
        con = sb("con", [P, C_COS2])
        ones = sb("ones", [P, P])
        pv = sb("pv", [P, DEPTH, 96])
        mod = sb("mod", [P, DEPTH, 48 * 2])
        mrow = sb("mrow", [P, CH])
        amp = sb("amp", [P, DEPTH + 1, 2, KD * 2])
        epsn = sb("epsn", [P, 2])
        zero2 = sb("zero2", [P, KD * 2])
        silc = sb("silc", [P, KD, 32])
        tmpc = sb("tmpc", [P, 2 * KD])
        sinks = sb("sinks", [P, 3, HEADS])
        nsink = sb("nsink", [P, 3, HEADS])
        wr = sb("wr", [P, KD, E])
        sq = sb("sq", [P, NT])
        rs = sb("rs", [P, NT])
        prob = sb("prob", [P, 2, NT])
        probT = sb("probT", [P, 2, NT])
        mxn = sb("mxn", [P, HEADS])
        nms = sb("nms", [P, 2, HEADS])
        lsum = sb("lsum", [P, 2, HEADS])
        sdif = sb("sdif", [P, HEADS])
        sexp = sb("sexp", [P, HEADS])
        route = sb("route", [P, 12 * E + QUAD])

        ident = con[:, C_ID:C_ID + P]
        h3 = hT[:].rearrange("p (k t) -> p k t", k=KD)
        m3 = merged[:].rearrange("p (k t) -> p k t", k=KD)
        tok = merged[:].rearrange("p (t d) -> p t d", t=6)
        q3 = qbuf[:].rearrange("p (k t) -> p k t", k=4)
        o4 = obuf[:].rearrange("p (b k t) -> p b k t", b=2, k=4)
        k3 = kbuf[:].rearrange("p (k t) -> p k t", k=2)
        v4 = vbuf[:, 0:2 * 6 * P].rearrange("p (b t f) -> p b t f", b=2, t=6)
        mod3 = mod[:].rearrange("p l (k w) -> p l k w", w=2)
        amp4 = amp[:].rearrange("p l n (k w) -> p l n k w", w=2)
        zero3 = zero2[:].rearrange("p (k w) -> p k w", w=2)
        q2a = qbuf[:, 0:4 * NX].rearrange("p (k t) -> p k t", k=4)
        q2b = merged[:, 8 * NX:12 * NX].rearrange("p (k t) -> p k t", k=4)
        sg2 = merged[:, 0:8 * NX].rearrange("p (k t) -> p k t", k=8)
        o2 = obuf[:, 0:8 * NX].rearrange("p (k t) -> p k t", k=8)
        k2b = obuf[:, 8 * NX:12 * NX].rearrange("p (k t) -> p k t", k=4)
        k2a = kbuf[:, 0:NX].rearrange("p (k t) -> p k t", k=1)
        v2 = vbuf[:].rearrange("p (t f) -> p t f", t=4)
        xs3 = hT[:, 0:KD * 3 * P].rearrange("p (k s) -> p k s", k=KD)
        hidT = hT[:, KD * 3 * P:2 * KD * 3 * P].rearrange("p (k s) -> p k s", k=KD)
        hid = qbuf[:].rearrange("p (h g f) -> p h g f", h=2, g=3)
        ye = obuf[:, 0:3 * D].rearrange("p (g d) -> p g d", g=3)
        selx = obuf[:, 3 * D:3 * D + 1024].rearrange("p (t s) -> p t s", t=4)
        selc = obuf[:, 4 * D:4 * D + 256].rearrange("p (t s) -> p t s", t=2)
        gselx = obuf[:, 4 * D + 256:5 * D + 256].rearrange("p (t s) -> p t s", t=4)
        gselc = obuf[:, 5 * D + 256:5 * D + 512].rearrange("p (t s) -> p t s", t=2)
        gTx = kbuf[:, 0:2 * NX].rearrange("p (g t) -> p g t", g=2)
        gTc = kbuf[:, 2 * NX:2 * NX + NC]
        gates3 = route[:, 6 * E:12 * E].rearrange("p (t e) -> p t e", t=6)
        work = prob[0:E, 1, :]
        selm = probT[0:E, 0, :]
        slotm = probT[0:E, 1, :]
        rone = sq[0:E, :]
        m8 = sexp[0:E, :]

        s_const, s_param, s_x, s_rope2, s_router, s_out = (sem(n) for n in (
            "const_loaded", "param_loaded0", "x_loaded", "rope2_loaded", "router_loaded", "out_stored"))
        s_param = [s_param, sem("param_loaded1")]
        w_full = [sem(f"weights_landed{i}") for i in range(RING)]
        full = [sem(f"psum_full{i}") for i in range(3)]
        free = [sem(f"psum_free{i}") for i in range(3)]
        set_full = [sem(f"set_full{i}") for i in range(2)] + [sem("turn_full")]
        set_free = [sem(f"set_free{i}") for i in range(2)] + [sem("turn_free")]
        act_step, dve_step = sem("act_step"), sem("dve_step")
        s_phase = sem("phase_done")
        slot_free = sem("slot_found_free")
        pv_ready = sem("param_turned")
        BANK = [0, 1024, 2048, 3072, 3584]
        SET = [0, 1536, 3072]
        TURN = 2

        def units_first(l, br):
            units = []
            streams = [("x", i) for i in range(NX // P)] + ([("c", i) for i in range(NC // P)] if l == 0 else [])
            for st, i in streams:
                q0 = i * P if st == "x" else NX + i * P
                for h in range(HEADS):
                    j, half = h % 4, h // 4
                    if st == "c":
                        segs, masks, lo, hi = [(512, NC, NX)], [], 512, 768
                        tiles = {512: 4, 640: 5}
                    elif br == 0:
                        segs, masks, lo, hi = [(0, NX, 0), (512, NC, NX)], [], 0, 768
                        tiles = {n * P: n for n in range(6)}
                    else:
                        a, b = max(0, i - 1), min(NX // P - 1, i + 1)
                        n = (b - a + 1) * P
                        lo, hi = 512 - n, 768
                        segs = [(lo, n, a * P), (512, NC, NX)]
                        masks = ([(lo, P, M_PREV)] if a < i else []) + ([(512 - P, P, M_NEXT)] if b > i else [])
                        tiles = {lo + n * P: a + n for n in range(b - a + 1)} | {512: 4, 640: 5}
                    units.append(dict(q0=q0, h=h, qt=q0 // P, j=j, half=half, kj=br, segs=segs, masks=masks, lo=lo,
                                      hi=hi, tiles=sorted(tiles.items()), vcol=half * HD))
            return units

        def units_second(br):
            units = []
            for i in range(NX // P):
                for h in range(HEADS):
                    if br == 0:
                        j, half, kj, vcol = h % 4, h // 4, 0, (h // 4) * HD
                        a = max(0, i - 1)
                        n = (i - a + 1) * P
                        masks = [(0, n, M_BAND + 2 * P - n)]
                    else:
                        j, half, kj, vcol = h // 2, h % 2, h // 2, P + h * HD
                        a, n = 0, (i + 1) * P
                        masks = [(0, n, M_DIL + 4 * P - n)]
                    units.append(dict(q0=i * P, h=h, qt=i, j=j, half=half, kj=kj, segs=[(0, n, a * P)], masks=masks,
                                      lo=0, hi=n, tiles=[(m * P, a + m) for m in range(n // P)], vcol=vcol))
            return units

        UNITS = {(l, br): units_first(l, br) for l in range(DEPTH) for br in range(2)}
        UNITS |= {(2, br): units_second(br) for br in range(2)}

        def attention_order(key):
            n = len(UNITS[key])
            order = []
            for s in range(n + 2):
                if 0 <= s - 1 < n:
                    order.append(("N", key, s - 1))
                if s < n:
                    order.append(("S", key, s))
                if 0 <= s - 1 < n:
                    order.append(("T", key, s - 1))
                if 0 <= s - 2 < n:
                    order.append(("V", key, s - 2))
                    if (s - 2) % HEADS == HEADS - 1:
                        order.append(("O", key, (s - 2) // HEADS))
            return order

        def pipelined(jobs):
            order, sums, rots = [], [], []
            for j in jobs:
                order.append(j)
                if rots:
                    order.append(rots.pop(0))
                if sums:
                    t = sums.pop(0)
                    order.append(("hs",) + t)
                    rots.append(("rot",) + t)
                if j[0] == "qk":
                    sums.append(j[1:])
            order += rots
            for t in sums:
                order += [("hs",) + t, ("rot",) + t]
            return order

        def plan_layer(l):
            first = [("qk", l, "ka"), ("v", l, 0), ("qk", l, "kb"), ("v", l, 1)]
            first += [("qk", l, f"qa{j}") for j in range(4)]
            first += [(f"conv_{w}", l, m) for hf in range(2) for w in "cxb" for m in (2 * hf, 2 * hf + 1)]
            gates = {br: [(w, l, br, d) for d in range(KD) for w in ("gate", "branch")] for br in range(3)}
            if l == 0:
                for br, vectors in ((2, [(0, i) for i in range(2, 6)]), (0, [(1, i) for i in range(3)]),
                                    (1, [(1, i) for i in range(3, 6)])):
                    for n, (m, i) in reversed(list(enumerate(vectors))):
                        gates[br][4 * n + 3:4 * n + 3] = [("adat", m, i)]
                        gates[br][4 * n + 1:4 * n + 1] = [("ada", m, i)]
            order = pipelined(first) + attention_order((l, 0))
            order += pipelined([("qk", l, f"qb{j}") for j in range(4)] + gates[2])
            order += attention_order((l, 1)) + gates[0] + gates[1]
            order += [("wout", l, d) for d in range(KD)]
            return order

        def plan_second():
            first = [("qk", 2, "ka"), ("v", 2, 0)] + [("qk", 2, f"qa{j}") for j in range(4)]
            first += [("qk", 2, f"kb{j}") for j in range(4)] + [("qk", 2, f"qb{j}") for j in range(4)]
            first += [("v", 2, 1), ("v", 2, 2)] + [("silg", 2, d) for d in range(8)]
            return (pipelined(first) + attention_order((2, 0)) + attention_order((2, 1))
                    + [("wout", 2, d) for d in range(KD)])

        PLAN = {0: plan_layer(0), 1: plan_layer(1), 2: plan_second()}
        PH = [(0, "mix"), (0, "ffn"), (1, "mix"), (1, "ffn"), (2, "mix")]
        FIRST = [(w, 0, i) for i in range(2) for w in ("ada", "adat")]
        every = FIRST + [j for n in range(3) for j in PLAN[n]]

        def of(*kinds):
            return [j for j in every if j[0] in kinds]

        def event(name, keys):
            return Count(sem(name), keys)

        sq_ready = event("square_ready", [("n",) + ph + (d,) for ph in PH for d in range(KD)])
        hpre = event("h_scaled", [ph + (d,) for ph in PH for d in range(KD)])
        h_ready = event("h_ready", [ph + (d,) for ph in PH for d in range(KD)])
        hs_of = {n: [j for j in PLAN[n] if j[0] == "hs"] for n in range(3)}
        rms_ready = event("root_ready", [("norm", 0, "mix")] + hs_of[0] + [("norm", 0, "ffn"), ("norm", 1, "mix")] + hs_of[1]
                          + [("norm", 1, "ffn"), ("norm", 2, "mix")] + hs_of[2])
        qsq_ready = event("head_square_ready", of("qk"))
        qn_ready = event("head_normed", of("hs"))
        q_ready = event("head_rotated", of("rot"))
        v_ready = event("values_ready", of("v"))
        cg_ready = event("conv_gate_copied", of("conv_c"))
        cu_used = event("conv_input_used", of("conv_x"))
        oc_ready = event("conv_ready", of("conv_b"))
        nm_ready = event("row_max_ready", of("S"))
        p_ready = event("exp_ready", of("S"))
        pn_ready = event("softmax_ready", of("N"))
        pt_ready = [event(f"expT_ready{r}", [j for j in of("T") if j[2] % 2 == r]) for r in range(2)]
        pv_done = event("values_summed", of("V"))
        oT_ready = event("outT_ready", of("O"))
        sig_ready = event("gate_sigmoid", of("gate", "silg"))
        gate_used = event("gate_used", of("branch", "silg"))
        ada_copied = event("modulation_copied", [("ada", l, i) for l in range(DEPTH) for i in range(6)])
        ada_done = event("modulation_ready", [("adat", l, i) for l in range(DEPTH) for i in range(6)])
        sil_sig = sem("cond_sigmoid")
        sil_ready = sem("cond_ready")
        aff_max, aff_exp = event("router_max", [0, 1]), event("router_exp", [0, 1])
        aff_ready = event("router_softmax", [0, 1])
        slots_ready = event("slots_ready", [0, 1])
        route_ready = event("route_ready", [0, 1])
        tok_ready = event("tok_ready", [0, 1])
        sel_ready, gT_ready, xs_ready = sem("selection_ready"), sem("gatesT_ready"), sem("expert_in_ready")
        hT_ready = sem("hidden_turned")
        eg_sig, hm_ready, y_ready = sem("expert_gate_sigmoid"), sem("expert_hidden"), sem("expert_out_copied")
        out_copied = event("out_copied", list(range(NX // P)))

        ROUNDS = E // QUAD

        job = {}
        used, parts = [0] * 3, [0] * 3
        turn = [0]

        SET_JOBS = [("eg", 0), ("eu", 0), ("eg", 1), ("eu", 1), ("in", 0), ("in", 1), ("in", 2), ("ed", 0), ("ed", 1),
                    ("in", 3), ("out", 0), ("out", 1), ("out", 2), ("out", 3)]
        PARTS = {"eg": 4, "eu": 4, "ed": 4, "in": 1, "out": 1}

        def turn_jobs(l):
            return [("gt", 0)] + ([("gt", 1)] if l == 0 else []) + [("ht", n) for n in range(4)]

        loop_job = {}
        first_in = {}
        loop_used, loop_parts = [0] * 3, [0] * 3
        for l in range(DEPTH):
            for n in range(4):
                t = n % 2
                loop_parts[t] += 1
                first_in[l, n] = (t, loop_used[t], loop_parts[t])
                loop_used[t] += 1
            js = [(k, n % 2, PARTS[k[0]]) for n, k in enumerate(SET_JOBS)] + [(k, TURN, 1) for k in turn_jobs(l)]
            per_job = [sum(1 for _, t, _ in js if t == u) for u in range(3)]
            per_part = [sum(p for _, t, p in js if t == u) for u in range(3)]
            u, f = list(loop_used), list(loop_parts)
            for k, t, p in js:
                f[t] += p
                loop_job[l, k] = (t, u[t], per_job[t], f[t], per_part[t])
                u[t] += 1
            for t in range(3):
                loop_used[t] += ROUNDS * per_job[t]
                loop_parts[t] += ROUNDS * per_part[t]

        chunks = []
        landed = [0] * RING
        chunk_at = []
        chunk_end = []
        chunk_key = {}

        def add_chunk(key, dmas):
            n = len(chunks)
            s = n % RING
            landed[s] += 16 * len(dmas)
            chunks.append(dmas)
            chunk_at.append((s, landed[s]))
            chunk_end.append(None)
            chunk_key[key] = n

        def cols(w, lo, n):
            return w[:, lo:lo + n].rearrange("(k p) f -> p k f", p=P)

        def ring3(s, k=8):
            return ring[:, s, :].rearrange("p (k f) -> p k f", k=k)

        def plain(w, lo):
            return [((slice(None), 8, slice(0, CH)), cols(w, lo, CH))]

        def paired(w, lo, jj):
            hs = [2 * jj, 4 + 2 * jj, 2 * jj + 1, 5 + 2 * jj]
            return [((slice(None), 8, slice(n * HD, (n + 1) * HD)), cols(w, lo + h * HD, HD)) for n, h in enumerate(hs)]

        ROUND = [(w, half, kk, pair) for w, half in [k for k in SET_JOBS if k[0] in ("eg", "eu", "ed")]
                 for kk in range(4) for pair in range(2)]
        EXPERT_W = {"eg": w_e_gate, "eu": w_e_up, "ed": w_e_down}
        assert len(ROUND) % RING == 0

        def expert_dst(s, e):
            return ring[:, s, e * 1024:(e + 1) * 1024].rearrange("p (k f) -> p k f", k=2)

        def expert_src(l, i, w, half, kk, e):
            at = i * (D * FH) + ((l * E + e) * D + kk * 2 * P) * FH + half * 512
            return bass.AP(EXPERT_W[w].tensor, at, [[FH, P], [P * FH, 2], [1, 512]])

        def chunk_of(j):
            kind, l, t = j[0], j[1], j[2]
            if kind == "qk":
                n = int(t[2:] or 0)
                if t[0] == "k" and l < 2:
                    return ("kv", l, "ab".index(t[1])), 0
                if l < 2:
                    return (t[:2], l, n // 2), n % 2
                return ("k2a", 0) if t == "ka" else ({"qa": "q2a", "kb": "k2b", "qb": "q2b"}[t[:2]], n // 2), n % 2
            if kind == "v":
                return ((("kv", l, t), 1) if l < 2 else (("k2a", 0), 1) if t == 0 else (("v2b", t - 1), 0))
            if kind[:4] == "conv":
                return (kind, l, t // 2), t % 2
            if kind == "gate":
                return ("gate", l, t, j[3] // 2), j[3] % 2
            if kind == "branch":
                return ("branch", l, t, j[3] // 4), j[3] % 4
            if kind == "silg":
                return ("g2a" if t < 4 else "g2b", t % 4 // 2), t % 2
            return (("wout", l, t // 2) if l < 2 else ("wout2", t // 2)), t % 2

        def chunk_dmas(key):
            name, l = key[0], key[1]
            if len(key) == 2:
                off = {"k2a": K2A, "k2b": K2B, "q2b": Q2B, "v2b": V2B, "g2a": G2A, "g2b": G2B}
                if name == "q2a":
                    return paired(w_in_2[0], Q2A, l)
                return plain(w_out_2[0], l * CH) if name == "wout2" else plain(w_in_2[0], off[name] + l * CH)
            n, wi = key[-1], w_in[l]
            if name == "ada":
                return plain(w_ada[l], n * CH)
            if name == "kv":
                return plain(wi, n * CH)
            if name in ("qa", "qb"):
                return paired(wi, OFF_QA if name == "qa" else OFF_QB, n)
            if name[:4] == "conv":
                return plain(wi, OFF_CONV + {"b": 0, "c": 512, "x": 1024}[name[5]] + n * CH)
            if name == "branch":
                return [((slice(None), 4, slice(0, 512)), cols(w_branch[l, key[2]], n * 512, 512))]
            if name == "gate":
                return plain(wi, OFF_GATE + key[2] * D + n * CH)
            return plain(w_out[l], n * CH)

        WEIGHTED = ("qk", "v", "conv_c", "conv_x", "conv_b", "gate", "branch", "silg", "wout")

        def chunk_keys(j):
            if j[0] == "ada":
                return [("ada", j[1], 4 * j[2] + g) for g in range(4)]
            return [chunk_of(j)[0]] if j[0] in WEIGHTED else []

        LOOPC = {}
        for n, jobs in enumerate((FIRST + PLAN[0], PLAN[1], PLAN[2])):
            for j in jobs:
                for key in chunk_keys(j):
                    if key not in chunk_key:
                        add_chunk(key, chunk_dmas(key))
            if n < DEPTH:
                LOOPC[n] = len(chunks)
                for i in range(ROUNDS):
                    for r, (w, half, kk, pair) in enumerate(ROUND):
                        add_chunk(("expert", n, i, r), [(None, expert_src(n, QUAD * i, w, half, kk, 2 * pair + e))
                                                        for e in range(2)])

        def load_params(eng, l):
            def param(dst, src):
                eng.dma_start(dst, src).then_inc(s_param[l], 16)

            def rows(r0, vec):
                n = vec.shape[0] // P
                param(prob[r0:r0 + n, l, 0:P], vec.rearrange("(k p) -> k p", p=P))

            rows(PB_ADA, b_ada[l])
            rows(PG_MIX, g_mix[l])
            rows(PG_FFN, g_ffn[l])
            param(prob[PCONV:PCONV + 12, l, 0:P], conv_w[l].rearrange("j (k p) -> (j k) p", p=P))
            for n, g in enumerate((qg_a, kg_a, qg_b, kg_b)):
                for r in range(2):
                    param(prob[PQK + n:PQK + n + 1, l, r * HD:(r + 1) * HD], g[l:l + 1, :])
            param(sinks[:, l, :], sink_b[l].partition_broadcast(P))
            if l == 0:
                rows(PEXTRA, c[0])
                rows(PEXTRA + 8, c_ctx)
            else:
                rows(PEXTRA, norm_gain_2[0])
                for n, g in enumerate((q_norm_a_2, k_norm_a_2, q_norm_b_2, k_norm_b_2)):
                    for r in range(2):
                        param(prob[PEXTRA + 8 + n:PEXTRA + 9 + n, 1, r * HD:(r + 1) * HD], g)
                param(sinks[:, 2, :], sinks_a_2[0].partition_broadcast(P))

        block = stack.enter_context(nc.Block())

        def width(l, name):
            return NT if l == 0 or (l == 1 and name in ("ka", "kb")) else NX

        def halves(w):
            return [(0, 512)] + ([(512, w)] if w > 512 else [])

        def qk_dest(l, name):
            if l < 2:
                return {"ka": k3[:, 0, :], "kb": k3[:, 1, :]}.get(name) if name[0] == "k" else q3[:, int(name[2]), :]
            return {"ka": k2a, "qa": q2a, "kb": k2b, "qb": q2b}[name[:2]][:, int(name[2:] or 0), :]

        def gain_col(l, name):
            n = ("qa", "ka", "qb", "kb").index(name[:2])
            return pv[:, l, PQK + n:PQK + n + 1] if l < 2 else pv[:, 1, PEXTRA + 8 + n:PEXTRA + 9 + n]

        def attn_bufs(key):
            l, br = key
            if l < 2:
                return q3, k3, lambda t, c0: v4[:, br, t, c0:c0 + HD]
            return (q2a, q2b)[br], (k2a, k2b)[br], lambda t, c0: v2[:, t, c0:c0 + HD]

        SEL = {0: 4, 1: 2}
        sel_base = {0: 0, 1: SEL[0] * (ROUNDS + 1)}
        PARAM_DMAS = (3 + 1 + 8 + 1 + 2, 3 + 1 + 8 + 1 + 1 + 8 + 1)

        def last_rot(key):
            return ("rot", key[0], "qb3" if key[1] else "qa3")

        def last_v(key):
            return ("v", key[0], 2 if key == (2, 1) else key[1])

        o_number = {j[1:]: n for n, j in enumerate(of("O"))}
        SINK = {(0, 1): 0, (1, 1): 1, (2, 0): 2}

        @block.tensor
        def _(pe):
            phases = [0]

            def meet():
                phases[0] += 1
                pe.sem_inc(s_phase, 1)
                pe.wait_ge(s_phase, 4 * phases[0])

            def begin(key, slot=None):
                if slot is None:
                    slot, turn[0] = turn[0], (turn[0] + 1) % 3
                n = used[slot]
                used[slot] += 1
                job[key] = [slot, n, None]
                if n:
                    pe.wait_ge(free[slot], n)
                return BANK[slot]

            def part(mm, key):
                slot = job[key][0]
                parts[slot] += 1
                mm.then_inc(full[slot], 1)
                job[key][2] = parts[slot]

            def weights(key):
                n = chunk_key[key]
                slot, value = chunk_at[n]
                pe.wait_ge(w_full[slot], value)
                return n, slot

            def need(ev, key):
                pe.wait_ge(ev.sem, ev.at[key])

            def norm_sum(ph, w):
                key = ("norm",) + ph
                b = begin(key)
                for d in range(KD):
                    need(sq_ready, ("n",) + ph + (d,))
                    for a, e in halves(w):
                        mm = pe.matmul(ps[:, b + a:b + e], ones[:, :], m3[:, d, a:e], start=d == 0, stop=d == KD - 1)
                part(mm, key)

            seen_h = set()

            def product(key, ph, lhs, rhs, w, nk):
                b = begin(key)
                for a, e in halves(w):
                    for k in range(nk):
                        if ph is not None and (ph, k) not in seen_h:
                            need(h_ready, ph + (k,))
                            seen_h.add((ph, k))
                        mm = pe.matmul(ps[:, b + a:b + e], lhs[:, k, :], rhs[:, k, a:e], start=k == 0, stop=k == nk - 1)
                part(mm, key)

            def run(j):
                kind, l = j[0], j[1]
                if kind in ("qk", "conv_c", "conv_x", "conv_b", "gate", "silg", "branch", "wout"):
                    ck, m = chunk_of(j)
                    cn, slot = weights(ck)
                    w = ring3(slot, 4 if kind == "branch" else 8)[:, :, m * P:(m + 1) * P]
                    wd = width(l, j[2] if kind == "qk" else "")
                    if kind == "branch":
                        br, d = j[2], j[3]
                        if d == 0 and br == 2:
                            need(oc_ready, ("conv_b", l, 3))
                        elif d == 0:
                            need(oT_ready, ("O", (l, br), len(UNITS[l, br]) // HEADS - 1))
                        product(j, None, w, o4[:, 0 if br == 0 else 1], wd, 4)
                    elif kind == "wout":
                        if j[2] == 0 and l < 2:
                            need(gate_used, ("branch", l, 1, KD - 1))
                        elif j[2] == 0:
                            need(oT_ready, ("O", (2, 0), NX // P - 1))
                            need(oT_ready, ("O", (2, 1), NX // P - 1))
                        product(j, None, w, m3 if l < 2 else o2, wd, KD)
                    else:
                        product(j, (l, "mix"), w, h3, wd, KD)
                    chunk_end[cn] = (full[job[j][0]], job[j][2])
                elif kind == "v":
                    ck, m = chunk_of(j)
                    cn, slot = weights(ck)
                    n, nt = (P, 6) if l < 2 else (P, 4) if j[2] == 0 else (CH, 4)
                    b = begin(j)
                    for t in range(nt):
                        for k in range(KD):
                            mm = pe.matmul(ps[:, b + t * n:b + (t + 1) * n], h3[:, k, t * P:(t + 1) * P],
                                           ring3(slot)[:, k, m * P:m * P + n], start=k == 0, stop=k == KD - 1)
                    part(mm, j)
                    chunk_end[cn] = (full[job[j][0]], job[j][2])
                elif kind == "ada":
                    if j == FIRST[0]:
                        pe.wait_ge(sil_ready, 1)
                    b = begin(j)
                    got = [weights(key) for key in chunk_keys(j)]
                    for k in range(KD):
                        for g, (_, slot) in enumerate(got):
                            mm = pe.matmul(ps[32 * g:32 * (g + 1), b:b + CH], silc[:, k, :], ring3(slot)[:, k, :],
                                           start=k == 0, stop=k == KD - 1, tile_position=(0, 32 * g))
                    part(mm, j)
                    for cn, _ in got:
                        chunk_end[cn] = (full[job[j][0]], job[j][2])
                elif kind == "adat":
                    need(ada_copied, ("ada",) + j[1:])
                    b = begin(j)
                    for n in range(2):
                        mm = pe.transpose(ps[:, b + n * P:b + (n + 1) * P], mrow[:, n * P:(n + 1) * P], ident)
                    part(mm, j)
                elif kind == "hs":
                    need(qsq_ready, ("qk",) + j[1:])
                    b = begin(j)
                    for a, e in halves(width(*j[1:])):
                        mm = pe.matmul(ps[:, b + a:b + e], con[:, C_HEAD:C_HEAD + P], sq[:, a:e], start=True, stop=True)
                    part(mm, j)
                elif kind == "rot":
                    need(qn_ready, ("hs",) + j[1:])
                    b = begin(j)
                    part(pe.matmul(ps[:, b:b + NX], con[:, C_ROT:C_ROT + P], qk_dest(*j[1:])[:, 0:NX],
                                   start=True, stop=True), j)
                elif kind == "S":
                    u = UNITS[j[1]][j[2]]
                    q, k, _ = attn_bufs(j[1])
                    if j[2] == 0:
                        need(q_ready, last_rot(j[1]))
                    b = begin(j, j[2] % 2)
                    r = slice(u["half"] * HD, (u["half"] + 1) * HD)
                    for n, (c0, w, k0) in enumerate(u["segs"]):
                        masks = u["masks"] if n == 0 else []
                        mm = pe.matmul(ps[:, b + c0:b + c0 + w], q[r, u["j"], u["q0"]:u["q0"] + P],
                                       k[r, u["kj"], k0:k0 + w], start=True, stop=not masks)
                        for i, (mc, mw, mask) in enumerate(masks):
                            mm = pe.matmul(ps[:, b + mc:b + mc + mw], ident, con[:, C_MASK + mask:C_MASK + mask + mw],
                                           start=False, stop=i == len(masks) - 1)
                    part(mm, j)
                elif kind == "T":
                    need(pn_ready, ("N",) + j[1:])
                    b = begin(j, 2)
                    for c0, _ in UNITS[j[1]][j[2]]["tiles"]:
                        mm = pe.transpose(ps[:, b + c0:b + c0 + P], prob[:, j[2] % 2, c0:c0 + P], ident)
                    part(mm, j)
                elif kind == "V":
                    u = UNITS[j[1]][j[2]]
                    v = attn_bufs(j[1])[2]
                    if j[2] == 0:
                        need(v_ready, last_v(j[1]))
                    need(pt_ready[j[2] % 2], ("T",) + j[1:])
                    n = o_number[j[1], j[2] // HEADS]
                    if u["h"] == 0 and n >= 2:
                        pe.wait_ge(oT_ready.sem, n - 1)
                    r = u["h"] % 2 * HD
                    b = BANK[3 + n % 2] + u["h"] // 2 * P
                    for i, (c0, t) in enumerate(u["tiles"]):
                        mm = pe.matmul(ps[r:r + HD, b:b + P], v(t, u["vcol"]), probT[:, j[2] % 2, c0:c0 + P],
                                       start=i == 0, stop=i == len(u["tiles"]) - 1, tile_position=(0, r))
                    mm.then_inc(pv_done.sem, 1)

            def experts(l):
                w = NT if l == 0 else NX
                nt = w // P
                key = ("router", l)
                b = begin(key)
                pe.wait_ge(s_router, 16 * (l + 1))
                for t in range(nt):
                    for k in range(KD):
                        if t == 0:
                            need(h_ready, (l, "ffn", k))
                        mm = pe.matmul(ps[:, b + t * E:b + (t + 1) * E], h3[:, k, t * P:(t + 1) * P], wr[:, k, :],
                                       start=k == 0, stop=k == KD - 1)
                part(mm, key)
                for t in range(nt):
                    if t == 2:
                        need(aff_ready, l)
                        b = begin(("affT", l))
                        for s in range(nt):
                            mm = pe.transpose(ps[0:E, b + s * P:b + (s + 1) * P], gates3[:, s, :], ident)
                        part(mm, ("affT", l))
                    b = begin(("tok", l, t))
                    for k in range(KD):
                        mm = pe.transpose(ps[:, b + k * P:b + (k + 1) * P], h3[:, k, t * P:(t + 1) * P], ident)
                    part(mm, ("tok", l, t))
                need(slots_ready, l)
                key = ("route", l)
                b = begin(key)
                for t in range(nt):
                    mm = pe.transpose(ps[:, b + t * E:b + (t + 1) * E], slotm[:, t * P:(t + 1) * P], ident[0:E, 0:E])
                part(mm, key)
                meet()
                groups = 3 if l == 0 else 2
                xs_base, half_base = (ROUNDS + 1) * 4 * l, ROUNDS * 2 * l

                def gather(b, n):
                    for d in (2 * n, 2 * n + 1):
                        o = b + d % 2 * 512
                        for t in range(4):
                            mm = pe.matmul(ps[:, o:o + 2 * P], tok[:, t, d * P:(d + 1) * P], selx[:, t, :],
                                           start=t == 0, stop=t == 3)
                        for t in range(2 if l == 0 else 0):
                            mm = pe.matmul(ps[:, o + 2 * P:o + 3 * P], tok[:, 4 + t, d * P:(d + 1) * P], selc[:, t, :],
                                           start=t == 0, stop=t == 1)
                    return mm

                pe.wait_ge(sel_ready, sel_base[l] + SEL[l])
                for n in range(4):
                    t, before, _ = first_in[l, n]
                    if before:
                        pe.wait_ge(set_free[t], before)
                    gather(SET[t], n).then_inc(set_full[t], 1)

                with pe.Fori(0, ROUNDS) as i:
                    def take(key):
                        t, n, per, _, _ = loop_job[l, key]
                        pe.wait_ge(set_free[t], i * per + n)
                        return SET[t]

                    def done(mm, key):
                        mm.then_inc(set_full[loop_job[l, key][0]], 1)

                    def experts_product(key, lhs):
                        w, half = key
                        b = take(key)
                        for kk in range(4):
                            slots = []
                            for pair in range(2):
                                slot, value = chunk_at[LOOPC[l] + ROUND.index((w, half, kk, pair))]
                                pe.wait_ge(w_full[slot], i * (32 * len(ROUND) // RING) + value)
                                slots.append(slot)
                                for k in (2 * kk, 2 * kk + 1):
                                    for e in range(2):
                                        s0 = pair * P + e * CX
                                        mm = pe.matmul(ps[e * CX:(e + 1) * CX, b + pair * 512:b + (pair + 1) * 512],
                                                       lhs[:, k, s0:s0 + CX], expert_dst(slot, e)[:, k % 2, :],
                                                       start=k == 0, stop=k == KD - 1, tile_position=(0, e * CX))
                            for k in (2 * kk, 2 * kk + 1) if l == 0 else ():
                                for e in range(QUAD):
                                    s0 = 2 * P + e * CC
                                    mm = pe.matmul(ps[e * CC:(e + 1) * CC, b + 1024:b + 1536], lhs[:, k, s0:s0 + CC],
                                                   expert_dst(slots[e // 2], e % 2)[:, k % 2, :],
                                                   start=k == 0, stop=k == KD - 1, tile_position=(0, e * CC))
                            done(mm, key)

                    def turn_hidden(n):
                        half = n // 2
                        pe.wait_ge(hm_ready, i * 2 + (1 + half + half_base))
                        b = take(("ht", n))
                        for f in range(2):
                            for g in range(groups):
                                o = b + f * 512 + g * P
                                f0 = (n % 2 * 2 + f) * P
                                mm = pe.transpose(ps[:, o:o + P], hid[:, half, g, f0:f0 + P], ident)
                        done(mm, ("ht", n))

                    def gather_next(n):
                        if n == 0:
                            pe.wait_ge(sel_ready, i * SEL[l] + (sel_base[l] + 2 * SEL[l]))
                        done(gather(take(("in", n)), n), ("in", n))

                    b = take(("gt", 0))
                    for g in range(2):
                        for t in range(4):
                            mm = pe.transpose(ps[:, b + (4 * g + t) * P:b + (4 * g + t + 1) * P],
                                              gselx[:, t, g * P:(g + 1) * P], ident)
                    done(mm, ("gt", 0))
                    pe.wait_ge(xs_ready, i * 4 + (4 + xs_base))
                    experts_product(("eg", 0), xs3)
                    if l == 0:
                        b = take(("gt", 1))
                        for t in range(2):
                            mm = pe.transpose(ps[:, b + t * P:b + (t + 1) * P], gselc[:, t, :], ident)
                        done(mm, ("gt", 1))
                    experts_product(("eu", 0), xs3)
                    experts_product(("eg", 1), xs3)
                    turn_hidden(0)
                    turn_hidden(1)
                    experts_product(("eu", 1), xs3)
                    gather_next(0)
                    turn_hidden(2)
                    gather_next(1)
                    turn_hidden(3)
                    gather_next(2)
                    pe.wait_ge(hT_ready, i * 4 + (4 + ROUNDS * 4 * l))
                    experts_product(("ed", 0), hidT)
                    experts_product(("ed", 1), hidT)
                    gather_next(3)
                    pe.wait_ge(gT_ready, i + (1 + ROUNDS * l))
                    pe.wait_ge(y_ready, i * 2 + (2 + half_base))
                    for n in range(4):
                        b = take(("out", n))
                        for d in (2 * n, 2 * n + 1):
                            o = b + d % 2 * 512
                            for g in range(2):
                                mm = pe.matmul(ps[:, o:o + NX], ye[:, g, d * P:(d + 1) * P], gTx[:, g, :],
                                               start=g == 0, stop=g == 1)
                            if l == 0:
                                o = b + 1024 + d % 2 * NC
                                mm = pe.matmul(ps[:, o:o + NC], ye[:, 2, d * P:(d + 1) * P], gTc, start=True, stop=True)
                        done(mm, ("out", n))
                for r in range(ROUNDS):
                    for n, (w, half, kk, _) in enumerate(ROUND):
                        t, _, _, f, per = loop_job[l, (w, half)]
                        chunk_end[LOOPC[l] + r * len(ROUND) + n] = (set_full[t], f - 3 + kk + r * per)
                meet()

            pe.wait_ge(s_x, 32)
            pe.wait_ge(s_const, 32)
            for d in range(KD):
                b = begin(("xT", d))
                for t in range(6):
                    mm = pe.transpose(ps[:, b + t * P:b + (t + 1) * P], tok[:, t, d * P:(d + 1) * P], ident)
                part(mm, ("xT", d))
            for l in range(DEPTH):
                pe.wait_ge(s_param[l], PARAM_DMAS[l] * 16)
                b = begin(("pv", l))
                rows = PROWS[l]
                part(pe.transpose(ps[:, b:b + rows], prob[0:rows, l, 0:P], ident[0:rows, 0:rows]), ("pv", l))
            meet()
            for j in FIRST:
                run(j)
            for l in range(DEPTH):
                norm_sum((l, "mix"), NT)
                for j in PLAN[l]:
                    run(j)
                meet()
                norm_sum((l, "ffn"), width(l, ""))
                experts(l)
            norm_sum((2, "mix"), NX)
            for j in PLAN[2]:
                run(j)
            meet()
            for t in range(NX // P):
                b = begin(("out", t))
                for k in range(KD):
                    mm = pe.transpose(ps[:, b + k * P:b + (k + 1) * P], xT[:, k, t * P:(t + 1) * P], ident)
                part(mm, ("out", t))

        @block.sync
        def _(sp):
            def load(n):
                slot = n % RING
                if n >= RING:
                    done, value = chunk_end[n - RING]
                    sp.wait_ge(done, value)
                for e, (at, src) in enumerate(chunks[n]):
                    if at is None:
                        dst = expert_dst(slot, e)
                    else:
                        _, k, cs = at
                        dst = ring3(slot, k)[:, :, cs]
                    sp.dma_start(dst, src).then_inc(w_full[slot], 16)

            def round_load(l, i, n, ahead):
                c = LOOPC[l] + n + ahead * len(ROUND)
                w, half, kk, pair = ROUND[n]
                done, value = chunk_end[c - RING]
                t = set_full.index(done)
                per_part = [j[4] for k, j in loop_job.items() if k[0] == l and j[0] == t][0]
                sp.wait_ge(done, i * per_part + value)
                sp.sem_inc(slot_free, 1)
                for e in range(2):
                    src = expert_src(l, i * QUAD, w, half, kk, QUAD * ahead + 2 * pair + e)
                    sp.dma_start(expert_dst(c % RING, e), src).then_inc(w_full[c % RING], 16)

            sp.dma_start(con[:, 0:C_ROT], consts[:, 0:C_ROT]).then_inc(s_const, 16)
            sp.dma_start(tok[:, 0:4, :], x[0].rearrange("(t p) d -> p t d", p=P)).then_inc(s_x, 16)
            sp.dma_start(tok[:, 4:6, :], ctx_in[0].rearrange("(t p) d -> p t d", p=P)).then_inc(s_x, 16)
            sp.dma_start(con[:, C_ROT:C_COS2], consts[:, C_ROT:C_COS2]).then_inc(s_const, 16)
            end = 0
            for l in range(DEPTH):
                for n in range(end, LOOPC[l] + RING):
                    load(n)
                with sp.Fori(0, ROUNDS - 1) as i:
                    for n in range(RING, len(ROUND)):
                        round_load(l, i, n, 0)
                    for n in range(RING):
                        round_load(l, i, n, 1)
                end = LOOPC[l] + ROUNDS * len(ROUND)
                for n in range(end - len(ROUND) + RING, end):
                    load(n)
            for n in range(end, len(chunks)):
                load(n)

        @block.gpsimd
        def _(pool):
            phases = [0]

            def meet():
                phases[0] += 1
                pool.sem_inc(s_phase, 1)
                pool.wait_ge(s_phase, 4 * phases[0])

            load_params(pool, 1)
            pool.dma_start(wr[:, :, :], w_router[0].rearrange("(k p) e -> p k e", p=P)).then_inc(s_router, 16)
            meet()
            for l in range(DEPTH):
                meet()
                meet()
                meet()
                if l == 0:
                    pool.dma_start(wr[:, :, :], w_router[1].rearrange("(k p) e -> p k e", p=P)).then_inc(s_router, 16)
                else:
                    pool.dma_start(con[:, C_COS:C_COS2], consts[:, C_COS2:C_END]).then_inc(s_rope2, 16)
            meet()
            for t in range(NX // P):
                pool.wait_ge(out_copied.sem, out_copied.at[t])
                pool.dma_start(out[0, t * P:(t + 1) * P, :], tok[:, t, :]).then_inc(s_out, 16)
            pool.wait_ge(s_out, 16 * (NX // P))

        class Engine:

            def __init__(self, eng, step_sem):
                self.eng, self.step, self.n, self.phases = eng, step_sem, 0, 0

            def do(self, ins, ev=None, key=None):
                if ev is None:
                    self.n += 1
                    ins.then_inc(self.step, 1)
                    self.eng.wait_ge(self.step, self.n)
                else:
                    ins.then_inc(ev.sem, 1)
                    self.eng.wait_ge(ev.sem, ev.at[key])

            def need(self, ev, key):
                self.eng.wait_ge(ev.sem, ev.at[key])

            def read(self, key):
                slot, _, value = job[key]
                self.eng.wait_ge(full[slot], value)
                return BANK[slot]

            def release(self, key):
                self.eng.sem_inc(free[job[key][0]], 1)

            def meet(self):
                self.phases += 1
                self.eng.sem_inc(s_phase, 1)
                self.eng.wait_ge(s_phase, 4 * self.phases)

        @block.scalar
        def _(act):
            A = Engine(act, act_step)
            sc = nc.scalar

            def func(o, i, f, **kw):
                return sc.activation(o, i, f, **kw)

            load_params(act, 0)
            for d in range(0, KD, 2):
                b = A.read(("xT", d))
                A.do(sc.copy(xT[:, d, :], ps[:, b:b + NT]))
                A.release(("xT", d))
            act.wait_ge(pv_ready, 1)
            func(tmpc[:, :], pv[:, 0, PEXTRA:PEXTRA + 2 * KD], ACT.Sigmoid).then_inc(sil_sig, 1)
            act.wait_ge(sil_sig, 1)
            A.meet()

            last_rs = [None]

            def root(key, w, n):
                b = A.read(key)
                A.do(func(rs[:, 0:w], ps[:, b:b + w], ACT.Sqrt, bias=epsn[:, n == D:(n == D) + 1]), rms_ready, key)
                A.release(key)

            def norm(ph, w):
                l = ph[0]
                for d in range(KD):
                    A.do(func(m3[:, d, 0:w], xT[:, d, 0:w], ACT.Square), sq_ready, ("n",) + ph + (d,))
                root(("norm",) + ph, w, D)
                last_rs[0] = (hpre, ph + (KD - 1,))
                sh = (SH1 if ph[1] == "mix" else SH2)
                if l < 2:
                    A.need(ada_done, ("adat", l, sh // KD))
                for d in range(KD):
                    A.need(hpre, ph + (d,))
                    for a, e in halves(w):
                        shift = zero3[:, d, 0:1] if l == 2 else mod3[:, l, sh + d, a // 512:a // 512 + 1]
                        ins = func(h3[:, d, a:e], h3[:, d, a:e], ACT.Identity, bias=shift)
                        if e == w:
                            A.do(ins, h_ready, ph + (d,))
                        else:
                            A.do(ins)

            last_hs, last_adat = [None], [None]

            def run(j):
                kind, l = j[0], j[1]
                if kind == "ada":
                    b = A.read(j)
                    if last_adat[0]:
                        A.read(last_adat[0])
                    A.do(sc.copy(mrow[:, :], ps[:, b:b + CH]), ada_copied, j)
                    A.release(j)
                elif kind == "adat":
                    last_adat[0] = j
                elif kind == "qk":
                    w = width(l, j[2])
                    b = A.read(j)
                    if last_hs[0]:
                        A.read(last_hs[0])
                    A.do(func(sq[:, 0:w], ps[:, b:b + w], ACT.Square), qsq_ready, j)
                    last_hs[0] = ("hs",) + j[1:]
                elif kind == "hs":
                    A.need(*last_rs[0])
                    root(j, width(*j[1:]), HD)
                elif kind == "rot":
                    last_rs[0] = (q_ready, j)
                elif kind == "v":
                    b = A.read(j)
                    if l < 2:
                        A.do(sc.copy(v4[:, j[2]], ps[:, b:b + NT].rearrange("p (t f) -> p t f", f=P)), v_ready, j)
                    else:
                        n, f0 = (P, 0) if j[2] == 0 else (CH, P + CH * (j[2] - 1))
                        A.do(sc.copy(v2[:, :, f0:f0 + n], ps[:, b:b + 4 * n].rearrange("p (t f) -> p t f", f=n)), v_ready, j)
                    A.release(j)
                elif kind == "conv_c":
                    w = width(l, "")
                    b = A.read(j)
                    if j[2] >= 2:
                        A.need(cu_used, ("conv_x", l, j[2] - 2))
                    A.do(sc.copy(prob[:, j[2] % 2, 0:w], ps[:, b:b + w]), cg_ready, j)
                    A.release(j)
                elif kind in ("gate", "silg"):
                    w = width(l, "")
                    n = j[3] if kind == "gate" else j[2]
                    b = A.read(j)
                    if kind == "gate" and n == 0 and j[2] in (2, 0):
                        A.need(pv_done, ("V", (l, 0 if j[2] == 2 else 1), len(UNITS[l, 0 if j[2] == 2 else 1]) - 1))
                    if kind == "gate" and n >= 2:
                        A.need(gate_used, ("branch", l, j[2], n - 2))
                    elif kind == "gate" and j[2] == 1:
                        A.need(gate_used, ("branch", l, 0, KD - 2 + n))
                    elif kind == "silg" and n >= 2:
                        A.need(gate_used, ("silg", l, n - 2))
                    A.do(func(probT[:, n % 2, 0:w], ps[:, b:b + w], ACT.Sigmoid), sig_ready, j)
                    if kind == "gate":
                        A.release(j)
                elif kind == "S":
                    u = UNITS[j[1]][j[2]]
                    lo, hi, h = u["lo"], u["hi"], u["h"]
                    b = A.read(j)
                    A.need(nm_ready, j)
                    if j[2] >= 2:
                        A.read(("T", j[1], j[2] - 2))
                    ins = func(prob[:, j[2] % 2, lo:hi], ps[:, b + lo:b + hi], ACT.Exp, bias=nms[:, u["qt"] % 2, h:h + 1],
                               scale=SCALE, accum_out=lsum[:, u["qt"] % 2, h:h + 1])
                    if j[1] in SINK:
                        A.do(ins)
                        A.do(func(sexp[:, h:h + 1], sinks[:, SINK[j[1]], h:h + 1], ACT.Exp,
                                  bias=nms[:, u["qt"] % 2, h:h + 1]), p_ready, j)
                    else:
                        A.do(ins, p_ready, j)
                    A.release(j)
                elif kind == "T" and j[2] % 2 == 0:
                    u = UNITS[j[1]][j[2]]
                    b = A.read(j)
                    if j[2] == 0 and j[1][1] == 1 and j[1][0] < 2:
                        A.need(gate_used, ("branch", j[1][0], 2, KD - 1))
                    elif j[2] == 0 and j[1] == (2, 0):
                        A.need(gate_used, ("silg", 2, KD - 1))
                    if j[2] >= 2:
                        A.need(pv_done, ("V", j[1], j[2] - 2))
                    A.do(sc.copy(probT[:, 0, u["lo"]:u["hi"]], ps[:, b + u["lo"]:b + u["hi"]]), pt_ready[0], j)
                    A.release(j)
                elif kind == "O" and j[1][0] < 2:
                    l, br = j[1]
                    A.need(pv_done, ("V", j[1], j[2] * HEADS + HEADS - 1))
                    b = BANK[3 + o_number[j[1:]] % 2]
                    if br == 1 and j[2] == 0:
                        A.read(("branch", l, 2, KD - 1))
                    A.do(sc.copy(o4[:, br, :, j[2] * P:(j[2] + 1) * P], ps[:, b:b + 512].rearrange("p (k t) -> p k t", k=4)),
                         oT_ready, j)

            def experts(l):
                w = width(l, "")
                A.need(aff_max, l)
                A.do(func(gates3[:, 0:w // P, :], gates3[:, 0:w // P, :], ACT.Exp), aff_exp, l)
                for t in range(w // P):
                    b = A.read(("tok", l, t))
                    A.do(sc.copy(tok[:, t, :], ps[:, b:b + D]))
                    A.release(("tok", l, t))
                A.meet()
                groups = 3 if l == 0 else 2
                half_base = ROUNDS * 2 * l

                def gathered(b, n, value):
                    sc.copy(xs3[:, 2 * n:2 * n + 2, 0:groups * P],
                            ps[:, b:b + 1024].rearrange("p (d s) -> p d s", d=2)[:, :, 0:groups * P]).then_inc(xs_ready, 1)
                    act.wait_ge(xs_ready, value)

                for n in range(4):
                    t, _, value = first_in[l, n]
                    act.wait_ge(set_full[t], value)
                    gathered(SET[t], n, n + 1 + (ROUNDS + 1) * 4 * l)
                    act.sem_inc(set_free[t], 1)

                with act.Fori(0, ROUNDS) as i:
                    def read(key):
                        t, _, _, f, per = loop_job[l, key]
                        act.wait_ge(set_full[t], i * per + f)
                        return SET[t]

                    def release(key):
                        act.sem_inc(set_free[loop_job[l, key][0]], 1)

                    def sigmoid(half):
                        b = read(("eg", half))
                        func(hid[:, half, 0:groups, :], ps[:, b:b + groups * 512].rearrange("p (g f) -> p g f", g=groups),
                             ACT.Sigmoid).then_inc(eg_sig, 1)
                        act.wait_ge(eg_sig, i * 2 + (1 + half + half_base))

                    def turned(n):
                        b = read(("ht", n))
                        sc.copy(hidT[:, 2 * n:2 * n + 2, 0:groups * P],
                                ps[:, b:b + 1024].rearrange("p (k s) -> p k s", k=2)[:, :, 0:groups * P]).then_inc(hT_ready, 1)
                        act.wait_ge(hT_ready, i * 4 + (1 + n + ROUNDS * 4 * l))
                        release(("ht", n))

                    def next_in(n):
                        b = read(("in", n))
                        gathered(b, n, i * 4 + (4 + n + 1 + (ROUNDS + 1) * 4 * l))
                        release(("in", n))

                    def output(half):
                        b = read(("ed", half))
                        sc.copy(ye[:, 0:groups, half * 512:(half + 1) * 512],
                                ps[:, b:b + groups * 512].rearrange("p (g f) -> p g f", g=groups)).then_inc(y_ready, 1)
                        act.wait_ge(y_ready, i * 2 + (1 + half + half_base))
                        release(("ed", half))

                    b = read(("gt", 0))
                    copied = sc.copy(gTx, ps[:, b:b + 1024].rearrange("p (g t) -> p g t", g=2))
                    if l == 0:
                        copied.then_inc(act_step, 1)
                        act.wait_ge(act_step, i + (A.n + 1))
                        release(("gt", 0))
                    else:
                        copied.then_inc(gT_ready, 1)
                        act.wait_ge(gT_ready, i + (1 + ROUNDS * l))
                        release(("gt", 0))
                    sigmoid(0)
                    if l == 0:
                        b = read(("gt", 1))
                        sc.copy(gTc, ps[:, b:b + NC]).then_inc(gT_ready, 1)
                        act.wait_ge(gT_ready, i + (1 + ROUNDS * l))
                        release(("gt", 1))
                    sigmoid(1)
                    turned(0)
                    turned(1)
                    next_in(0)
                    turned(2)
                    next_in(1)
                    turned(3)
                    next_in(2)
                    output(0)
                    output(1)
                    next_in(3)
                if l == 0:
                    A.n += ROUNDS
                A.meet()

            for j in FIRST:
                run(j)
            for l in range(DEPTH):
                norm((l, "mix"), NT)
                for j in PLAN[l]:
                    run(j)
                A.meet()
                norm((l, "ffn"), width(l, ""))
                experts(l)
            norm((2, "mix"), NX)
            for j in PLAN[2]:
                run(j)
            A.meet()
            for t in range(NX // P):
                b = A.read(("out", t))
                A.do(sc.copy(tok[:, t, :], ps[:, b:b + D]), out_copied, t)
                A.release(("out", t))

        @block.vector
        def _(dve):
            V = Engine(dve, dve_step)
            v = nc.vector

            V.do(v.memset(ones[:, :], 1.0))
            V.do(v.memset(route[:, :], 0.0))
            V.do(v.memset(epsn[:, 0:1], HD * EPS))
            V.do(v.memset(epsn[:, 1:2], D * EPS))
            V.do(v.memset(zero2[:, :], 0.0))
            V.do(v.memset(silc[:, :, :], 0.0))
            for d in range(1, KD, 2):
                b = V.read(("xT", d))
                V.do(v.tensor_copy(xT[:, d, :], ps[:, b:b + NT]))
                V.release(("xT", d))
            for l in range(DEPTH):
                b = V.read(("pv", l))
                if l == 0:
                    v.tensor_copy(pv[:, l, 0:PROWS[l]], ps[:, b:b + PROWS[l]]).then_inc(pv_ready, 1)
                    dve.wait_ge(pv_ready, 1)
                else:
                    V.do(v.tensor_copy(pv[:, l, 0:PROWS[l]], ps[:, b:b + PROWS[l]]))
                V.release(("pv", l))
                V.do(v.tensor_scalar(pv[:, l, PQK:PQK + 4], pv[:, l, PQK:PQK + 4], HD ** 0.5, None, ALU.mult))
            V.do(v.tensor_scalar(pv[:, 1, PEXTRA + 8:PEXTRA + 12], pv[:, 1, PEXTRA + 8:PEXTRA + 12], HD ** 0.5, None, ALU.mult))
            V.do(v.tensor_scalar(nsink[:, :, :], sinks[:, :, :], -1.0, None, ALU.mult))
            dve.wait_ge(sil_sig, 1)
            V.do(v.tensor_tensor(silc[:, :, 0], tmpc[:, 0:KD], pv[:, 0, PEXTRA:PEXTRA + KD], ALU.mult))
            v.tensor_tensor(silc[:, :, 1], tmpc[:, KD:2 * KD], pv[:, 0, PEXTRA + KD:PEXTRA + 2 * KD],
                            ALU.mult).then_inc(sil_ready, 1)
            dve.wait_ge(sil_ready, 1)
            V.meet()

            def modulation(j):
                l, i = j[1], j[2]
                b = V.read(j)
                turned = ps[:, b:b + CH].rearrange("p (h g z) -> p h g z", h=2, g=4)[:, :, :, 0:2]
                vector = mod3[:, l, KD * i:KD * (i + 1), :].rearrange("p (g h) w -> p h g w", h=2)
                bias = pv[:, l, PB_ADA + KD * i:PB_ADA + KD * (i + 1)].rearrange("p (g h) -> p h g", h=2)
                ins = v.tensor_tensor(vector, turned, bias.unsqueeze(3).broadcast_to([P, 2, 4, 2]), ALU.add)
                V.do(ins, ada_done, j)
                V.release(j)
                for n, (sc_, g) in enumerate(((SC1, PG_MIX), (SC2, PG_FFN))):
                    if KD * i == sc_:
                        gain = pv[:, l, g:g + KD].unsqueeze(2).broadcast_to([P, KD, 2])
                        V.do(v.scalar_tensor_tensor(amp4[:, l, n], mod3[:, l, sc_:sc_ + KD, :], 1.0, gain, ALU.add, ALU.mult))
                        V.do(v.tensor_scalar(amp4[:, l, n], amp4[:, l, n], D ** 0.5, None, ALU.mult))

            def norm(ph, w):
                key = ("norm",) + ph
                V.need(rms_ready, key)
                V.do(v.reciprocal(rs[:, 0:w], rs[:, 0:w]))
                for d in range(KD):
                    for a, e in halves(w):
                        ins = v.scalar_tensor_tensor(h3[:, d, a:e], xT[:, d, a:e],
                                                     amp4[:, ph[0], ph[1] == "ffn", d, a // 512:a // 512 + 1],
                                                     rs[:, a:e], ALU.mult, ALU.mult)
                        if e == w:
                            V.do(ins, hpre, ph + (d,))
                        else:
                            V.do(ins)

            def run(j):
                kind, l = j[0], j[1]
                w = width(l, j[2] if kind in ("qk", "hs") else "") if kind not in ("S", "N", "T", "V", "O") else 0
                if kind == "adat":
                    modulation(j)
                elif kind == "qk":
                    b = V.read(j)
                    V.need(qsq_ready, j)
                    V.do(v.tensor_copy(qk_dest(*j[1:])[:, 0:w], ps[:, b:b + w]))
                    V.release(j)
                elif kind == "hs":
                    V.need(rms_ready, j)
                    V.do(v.reciprocal(rs[:, 0:w], rs[:, 0:w]))
                    t = qk_dest(*j[1:])[:, 0:w]
                    V.do(v.scalar_tensor_tensor(t, t, gain_col(*j[1:]), rs[:, 0:w], ALU.mult, ALU.mult), qn_ready, j)
                elif kind == "rot":
                    t = qk_dest(*j[1:])[:, 0:NX]
                    b = V.read(j)
                    V.do(v.tensor_tensor(rs[:, 0:NX], ps[:, b:b + NX], con[:, C_SIN:C_SIN + NX], ALU.mult))
                    V.release(j)
                    V.do(v.tensor_tensor(t, t, con[:, C_COS:C_COS + NX], ALU.mult))
                    V.do(v.tensor_tensor(t, t, rs[:, 0:NX], ALU.add), q_ready, j)
                elif kind == "conv_x":
                    m = j[2]
                    u, y = prob[:, m % 2], o4[:, 1, m]
                    tap = [pv[:, l, PCONV + 4 * t + m:PCONV + 4 * t + m + 1] for t in range(3)]
                    V.need(cg_ready, ("conv_c", l, m))
                    b = V.read(j)
                    V.do(v.tensor_tensor(u[:, 0:w], u[:, 0:w], ps[:, b:b + w], ALU.mult))
                    V.release(j)
                    V.do(v.tensor_scalar(y[:, 0:w], u[:, 0:w], tap[1], None, ALU.mult))
                    for a, e in halves(w):
                        V.do(v.scalar_tensor_tensor(y[:, a + 1:e], u[:, a:e - 1], tap[0], y[:, a + 1:e], ALU.mult, ALU.add))
                        ins = v.scalar_tensor_tensor(y[:, a:e - 1], u[:, a + 1:e], tap[2], y[:, a:e - 1], ALU.mult, ALU.add)
                        if e == w:
                            V.do(ins, cu_used, j)
                        else:
                            V.do(ins)
                elif kind == "conv_b":
                    y = o4[:, 1, j[2]]
                    b = V.read(j)
                    V.do(v.tensor_tensor(y[:, 0:w], y[:, 0:w], ps[:, b:b + w], ALU.mult), oc_ready, j)
                    V.release(j)
                elif kind == "branch":
                    br, d = j[2], j[3]
                    g = probT[:, d % 2, 0:w]
                    V.need(sig_ready, ("gate", l, br, d))
                    b = V.read(j)
                    if br == 2:
                        V.do(v.tensor_tensor(m3[:, d, 0:w], g, ps[:, b:b + w], ALU.mult), gate_used, j)
                        V.release(j)
                    else:
                        V.do(v.tensor_tensor(g, g, ps[:, b:b + w], ALU.mult))
                        V.release(j)
                        V.do(v.tensor_tensor(m3[:, d, 0:w], m3[:, d, 0:w], g, ALU.add), gate_used, j)
                elif kind == "silg":
                    d = j[2]
                    g = probT[:, d % 2, 0:w]
                    V.need(sig_ready, j)
                    b = V.read(j)
                    V.do(v.tensor_tensor(sg2[:, d, :], g, ps[:, b:b + w], ALU.mult), gate_used, j)
                    V.release(j)
                elif kind == "wout":
                    d = j[2]
                    b = V.read(j)
                    for a, e in halves(w):
                        if l < 2:
                            V.do(v.scalar_tensor_tensor(xT[:, d, a:e], ps[:, b + a:b + e],
                                                        mod3[:, l, GT1 + d, a // 512:a // 512 + 1], xT[:, d, a:e],
                                                        ALU.mult, ALU.add))
                        else:
                            V.do(v.tensor_tensor(xT[:, d, a:e], xT[:, d, a:e], ps[:, b + a:b + e], ALU.add))
                    V.release(j)
                elif kind == "S":
                    u = UNITS[j[1]][j[2]]
                    h, p2 = u["h"], u["qt"] % 2
                    b = V.read(j)
                    V.do(v.tensor_reduce(mxn[:, h:h + 1], ps[:, b + u["lo"]:b + u["hi"]], AX.X, ALU.max, negate=True))
                    if j[1] in SINK:
                        V.do(v.tensor_scalar(nms[:, p2, h:h + 1], mxn[:, h:h + 1], SCALE, nsink[:, SINK[j[1]], h:h + 1],
                                             ALU.mult, ALU.min), nm_ready, j)
                    else:
                        V.do(v.tensor_scalar(nms[:, p2, h:h + 1], mxn[:, h:h + 1], SCALE, None, ALU.mult), nm_ready, j)
                elif kind == "N":
                    u = UNITS[j[1]][j[2]]
                    h = u["h"]
                    V.need(p_ready, ("S",) + j[1:])
                    den, p_ = lsum[:, u["qt"] % 2, h:h + 1], prob[:, j[2] % 2, u["lo"]:u["hi"]]
                    if j[1] in SINK:
                        V.do(v.tensor_tensor(den, den, sexp[:, h:h + 1], ALU.add))
                    V.do(v.reciprocal(den, den))
                    V.do(v.tensor_scalar(p_, p_, den, None, ALU.mult), pn_ready, j)
                elif kind == "T" and j[2] % 2 == 1:
                    u = UNITS[j[1]][j[2]]
                    b = V.read(j)
                    if j[2] >= 2:
                        V.need(pv_done, ("V", j[1], j[2] - 2))
                    V.do(v.tensor_copy(probT[:, 1, u["lo"]:u["hi"]], ps[:, b + u["lo"]:b + u["hi"]]), pt_ready[1], j)
                    V.release(j)
                elif kind == "O" and j[1][0] == 2:
                    V.need(pv_done, ("V", j[1], j[2] * HEADS + HEADS - 1))
                    b = BANK[3 + o_number[j[1:]] % 2]
                    t0 = 4 * j[1][1]
                    tt = slice(j[2] * P, (j[2] + 1) * P)
                    V.do(v.tensor_tensor(o2[:, t0:t0 + 4, tt], sg2[:, t0:t0 + 4, tt],
                                         ps[:, b:b + 512].rearrange("p (k t) -> p k t", k=4), ALU.mult), oT_ready, j)

            def experts(l):
                w = width(l, "")
                segs = halves(w)
                nt = w // P
                b = V.read(("router", l))
                logits = ps[:, b:b + nt * E].rearrange("p (t e) -> p t e", t=nt)
                gates = gates3[:, 0:nt, :]

                def of_token(stat):
                    return stat[:, 0:nt].unsqueeze(2).broadcast_to([P, nt, E])

                V.do(v.tensor_reduce(mxn[:, 0:nt], logits, AX.X, ALU.max))
                V.do(v.tensor_tensor(gates, logits, of_token(mxn), ALU.subtract), aff_max, l)
                V.release(("router", l))
                V.do(v.memset(rone[:, 0:w], 1.0))
                V.need(aff_exp, l)
                V.do(v.tensor_reduce(sdif[:, 0:nt], gates, AX.X, ALU.add))
                V.do(v.reciprocal(sdif[:, 0:nt], sdif[:, 0:nt]))
                V.do(v.tensor_tensor(gates, gates, of_token(sdif), ALU.mult), aff_ready, l)
                b = V.read(("affT", l))
                V.do(v.tensor_copy(work[:, 0:w], ps[0:E, b:b + w]))
                V.release(("affT", l))
                for n, (a, e) in enumerate(segs):
                    for _ in range((CX, CC)[n] // 8):
                        V.do(v.max(m8[:, :], work[:, a:e]))
                        V.do(v.match_replace(work[:, a:e], m8[:, :], work[:, a:e], -1.0))
                V.do(v.tensor_scalar(selm[:, 0:w], work[:, 0:w], 0.0, None, ALU.is_lt))
                for a, e in segs:
                    V.do(v.tensor_tensor_scan(slotm[:, a:e], rone[:, a:e], selm[:, a:e], 0.0, ALU.mult, ALU.add))
                V.do(v.tensor_tensor(slotm[:, 0:w], slotm[:, 0:w], selm[:, 0:w], ALU.mult))
                V.do(v.tensor_scalar(slotm[:, 0:w], slotm[:, 0:w], -1.0, None, ALU.add), slots_ready, l)
                key = ("route", l)
                b = V.read(key)
                V.do(v.tensor_copy(route[:, 0:nt * E], ps[:, b:b + nt * E]))
                V.release(key)
                V.meet()
                groups = 3 if l == 0 else 2
                half_base = ROUNDS * 2 * l
                per_round = 2 + KD * len(segs)

                def four_of(n, t0, tiles, e0):
                    lo = (6 * n + t0) * E
                    return bass.AP(route[:, :].tensor, e0 + lo, [[12 * E + QUAD, P], [E, tiles], [1, QUAD]])

                def select(e0, before):
                    n = 0
                    for tiles, t0, cap, sel, gsel in ((4, 0, CX, selx, gselx), (2, 4, CC, selc, gselc))[:2 - l]:
                        shape = [P, tiles, QUAD, cap]
                        s4 = sel.rearrange("p t (e c) -> p t e c", e=QUAD)
                        g4 = gsel.rearrange("p t (e c) -> p t e c", e=QUAD)
                        slot, gate = (four_of(n_, t0, tiles, e0).unsqueeze(3).broadcast_to(shape) for n_ in range(2))
                        iota = con[:, C_IOTA:C_IOTA + cap].unsqueeze(1).unsqueeze(1).broadcast_to(shape)
                        v.tensor_tensor(s4, iota, slot, ALU.is_equal).then_inc(sel_ready, 1)
                        dve.wait_ge(sel_ready, before + (n + 1))
                        v.tensor_tensor(g4, s4, gate, ALU.mult).then_inc(sel_ready, 1)
                        dve.wait_ge(sel_ready, before + (n + 2))
                        n += 2

                select(0, sel_base[l])
                for n in range(4):
                    t, _, value = first_in[l, n]
                    dve.wait_ge(set_full[t], value)
                with dve.Fori(0, ROUNDS) as i:
                    count = [0]

                    def step(ins):
                        count[0] += 1
                        ins.then_inc(dve_step, 1)
                        dve.wait_ge(dve_step, i * per_round + (V.n + count[0]))

                    def read(key):
                        t, _, _, f, per = loop_job[l, key]
                        dve.wait_ge(set_full[t], i * per + f)
                        return SET[t]

                    def release(key):
                        dve.sem_inc(set_free[loop_job[l, key][0]], 1)

                    def banks(key):
                        b = read(key)
                        return ps[:, b:b + groups * 512].rearrange("p (g f) -> p g f", g=groups)

                    def hidden(half):
                        g = hid[:, half, 0:groups, :]
                        dve.wait_ge(eg_sig, i * 2 + (1 + half + half_base))
                        step(v.tensor_tensor(g, g, banks(("eg", half)), ALU.mult))
                        release(("eg", half))
                        v.tensor_tensor(g, g, banks(("eu", half)), ALU.mult).then_inc(hm_ready, 1)
                        dve.wait_ge(hm_ready, i * 2 + (1 + half + half_base))
                        release(("eu", half))

                    hidden(0)
                    read(turn_jobs(l)[1 - l])
                    select(i * QUAD + QUAD, i * SEL[l] + (sel_base[l] + SEL[l]))
                    hidden(1)
                    for n in range(4):
                        b = read(("out", n))
                        for d in (2 * n, 2 * n + 1):
                            for a, e in segs:
                                o = b + d % 2 * 512 if a == 0 else b + 1024 + d % 2 * NC
                                step(v.scalar_tensor_tensor(xT[:, d, a:e], ps[:, o:o + e - a],
                                                            mod3[:, l, GT2 + d, a // 512:a // 512 + 1], xT[:, d, a:e],
                                                            ALU.mult, ALU.add))
                        release(("out", n))
                    assert count[0] == per_round, count
                V.n += ROUNDS * per_round
                V.meet()

            for j in FIRST:
                run(j)
            for l in range(DEPTH):
                norm((l, "mix"), NT)
                for j in PLAN[l]:
                    run(j)
                V.meet()
                norm((l, "ffn"), width(l, ""))
                experts(l)
            V.do(v.tensor_scalar(amp4[:, 2, 0, :, 0], pv[:, 1, PEXTRA:PEXTRA + KD], D ** 0.5, None, ALU.mult))
            dve.wait_ge(s_rope2, 16)
            norm((2, "mix"), NX)
            for j in PLAN[2]:
                run(j)
            V.meet()


_INS = ["x", "c", "ctx", "c_ctx", "w_ada", "b_ada", "g_mix", "g_ffn", "w_in", "qg_a", "kg_a", "qg_b", "kg_b", "sink_b",
        "conv_w", "w_branch", "w_out", "w_router", "w_e_gate", "w_e_up", "w_e_down", "norm_gain_2", "w_in_2",
        "q_norm_a_2", "k_norm_a_2", "sinks_a_2", "q_norm_b_2", "k_norm_b_2", "w_out_2"]


def kernel(**inputs):
    import concourse.bacc as bacc
    from concourse.bass_utils import run_bass_kernel_spmd

    nc = bacc.Bacc("TRN2", target_bir_lowering=False, num_devices=1)
    arrays, args = {}, []
    for name in _INS + ["consts"]:
        a = constants() if name == "consts" else np.ascontiguousarray(inputs[name])
        arrays[f"in_{name}"] = a
        args.append(nc.dram_tensor(f"in_{name}", a.shape, mybir.dt.from_np(a.dtype), kind="ExternalInput").ap())
    args.append(nc.dram_tensor("out_x", (1, NX, D), F32, kind="ExternalOutput").ap())
    program(nc, *args)
    return run_bass_kernel_spmd(nc, [arrays], core_ids=[0]).results[0]["out_x"]
```
